# Optimizing a Trainium2 kernel written in Bass

```python
import jax
import jax.numpy as jnp
from jax import lax
import numpy as np

D_MODEL = 1024
BATCH = 1
SEQ = 128
DEPTH = 2
DEC_BATCH = 1
DEC_SEQ = 512
PAST_LEN = 128

GRID_W = 64
N_EVEN = (DEPTH + 1) // 2
N_ODD = DEPTH // 2
CHUNK = 128
Q_BLOCK = 128
EPS = 1e-6
RET_HEADS = 8
RET_DK = 64
RET_DV = 128
RET_Q = RET_HEADS * RET_DK
RET_V = RET_HEADS * RET_DV
SSM_D_INNER = 1024
SSM_HEADDIM = 64
SSM_HEADS = SSM_D_INNER // SSM_HEADDIM
SSM_GROUPS = 4
SSM_RATIO = SSM_HEADS // SSM_GROUPS
SSM_STATE = 128
SSM_XBC = SSM_D_INNER + 2 * SSM_GROUPS * SSM_STATE
HYB_IN = 2 * RET_Q + 2 * RET_V + SSM_D_INNER + SSM_XBC + SSM_HEADS
HYB_MIX = RET_V + SSM_D_INNER
ATT_HEADS = 16
ATT_KV_HEADS = 4
ATT_RATIO = ATT_HEADS // ATT_KV_HEADS
ATT_HD = 64
ATT_QKV = (ATT_HEADS + 2 * ATT_KV_HEADS) * ATT_HD
ROT_FREQS = ATT_HD // 4
ROPE_BASE = 10000.0
FFN_HIDDEN = 2816

kernel_name = 'hybrid_retention_ssd_gqa_prefix_dit_step'

def rms_norm(x):
    xf = x.astype(jnp.float32)
    return (xf * lax.rsqrt(jnp.mean(xf * xf, axis=-1, keepdims=True) + EPS)).astype(x.dtype)

def head_layer_norm(x):
    xf = x.astype(jnp.float32)
    mu = jnp.mean(xf, axis=-1, keepdims=True)
    var = jnp.mean(jnp.square(xf - mu), axis=-1, keepdims=True)
    return ((xf - mu) * lax.rsqrt(var + EPS)).astype(x.dtype)

def dwconv3(x, w, b):
    xp = jnp.pad(x, ((0, 0), (1, 1), (0, 0)))
    return xp[:, :-2] * w[0] + xp[:, 1:-1] * w[1] + xp[:, 2:] * w[2] + b

def grid_rope_angles(L):
    rows = L // GRID_W
    row = jnp.repeat(jnp.arange(rows, dtype=jnp.float32), GRID_W)
    col = jnp.tile(jnp.arange(GRID_W, dtype=jnp.float32), rows)
    inv = ROPE_BASE ** (-jnp.arange(ROT_FREQS, dtype=jnp.float32) / ROT_FREQS)
    ang = jnp.stack([row[:, None] * inv, col[:, None] * inv], axis=1)
    return jnp.cos(ang), jnp.sin(ang)

def apply_rope(x, cos, sin):
    b, L, h, d = x.shape
    xr = x.astype(jnp.float32).reshape(b, L, h, 2, 2, ROT_FREQS)
    x1, x2 = xr[..., 0, :], xr[..., 1, :]
    c, s = cos[None, :, None], sin[None, :, None]
    out = jnp.stack([x1 * c - x2 * s, x1 * s + x2 * c], axis=-2)
    return out.reshape(b, L, h, d).astype(x.dtype)

def chunked_decay_scan(q, k, v, log_a, s0):
    f32 = jnp.float32
    b, L, g, dk = q.shape
    r, dv = v.shape[3], v.shape[4]
    n = L // CHUNK

    def chunks(t):
        return jnp.moveaxis(t.astype(f32).reshape((b, n, CHUNK) + t.shape[2:]), 1, 0)

    lower = jnp.tril(jnp.ones((CHUNK, CHUNK), dtype=bool))

    def step(s, inp):
        qc, kc, vc, ac = inp
        cum = jnp.cumsum(ac, axis=1)
        cum_t = jnp.moveaxis(cum, 1, -1)
        decay = jnp.exp(jnp.where(lower, cum_t[..., :, None] - cum_t[..., None, :], -jnp.inf))
        scores = jnp.einsum('bigd,bjgd->bgij', qc, kc)
        y = jnp.einsum('bgij,bgrij,bjgrv->bigrv', scores, decay, vc)
        y = y + jnp.einsum('bigd,bgrdv->bigrv', qc, s) * jnp.exp(cum)[..., None]
        last = cum_t[..., -1:]
        w = jnp.exp(last - cum_t)
        s = s * jnp.exp(last)[..., None] + jnp.einsum('bjgd,bjgrv,bgrj->bgrdv', kc, vc, w)
        return s, y

    s_fin, ys = lax.scan(step, s0.astype(f32), (chunks(q), chunks(k), chunks(v), chunks(log_a)))
    y = jnp.moveaxis(ys, 0, 1).reshape(b, L, g, r, dv)
    return y.astype(q.dtype), s_fin.astype(s0.dtype)

def hybrid_mixer(h, s_ret0, s_ssm0, w_in, w_out, log_decay, gn_gain, conv_w, conv_b,
                 a_log, dt_bias, d_skip, norm_gain):
    b, L, _ = h.shape
    cuts = np.cumsum([RET_Q, RET_Q, RET_V, RET_V, SSM_D_INNER, SSM_XBC]).tolist()
    q, k, v, g, z, xbc, dt_raw = jnp.split(h @ w_in, cuts, axis=-1)
    q = q.reshape(b, L, RET_HEADS, RET_DK)
    k = k.reshape(b, L, RET_HEADS, RET_DK) * (RET_DK ** -0.5)
    v = v.reshape(b, L, RET_HEADS, 1, RET_DV)
    xbc = jax.nn.silu(dwconv3(xbc, conv_w, conv_b))
    xs, bm, cm = jnp.split(xbc, [SSM_D_INNER, SSM_D_INNER + SSM_GROUPS * SSM_STATE], axis=-1)
    xs = xs.reshape(b, L, SSM_HEADS, SSM_HEADDIM)
    bm = bm.reshape(b, L, SSM_GROUPS, SSM_STATE)
    cm = cm.reshape(b, L, SSM_GROUPS, SSM_STATE)
    ret_ys, ret_fin, ssm_ys, ssm_fin = [], [], [], []
    for d in range(2):
        fl = (lambda t: t) if d == 0 else (lambda t: jnp.flip(t, axis=1))
        la_ret = jnp.broadcast_to(log_decay[d].astype(jnp.float32)[:, None], (b, L, RET_HEADS, 1))
        y, s = chunked_decay_scan(fl(q), fl(k), fl(v), la_ret, s_ret0[:, d][:, :, None])
        ret_ys.append(fl(y))
        ret_fin.append(s.reshape(b, RET_HEADS, RET_DK, RET_DV))
        dt = jax.nn.softplus((dt_raw + dt_bias[d]).astype(jnp.float32))
        la_ssm = (dt * -jnp.exp(a_log[d].astype(jnp.float32))).reshape(b, L, SSM_GROUPS, SSM_RATIO)
        v_ssm = (xs * dt[..., None]).reshape(b, L, SSM_GROUPS, SSM_RATIO, SSM_HEADDIM)
        s0 = s_ssm0[:, d].reshape(b, SSM_GROUPS, SSM_RATIO, SSM_STATE, SSM_HEADDIM)
        y, s = chunked_decay_scan(fl(cm), fl(bm), fl(v_ssm), fl(la_ssm), s0)
        ssm_ys.append(fl(y).reshape(b, L, SSM_HEADS, SSM_HEADDIM) + d_skip[d][:, None] * xs)
        ssm_fin.append(s.reshape(b, SSM_HEADS, SSM_STATE, SSM_HEADDIM))
    y_ret = head_layer_norm((ret_ys[0] + ret_ys[1]).reshape(b, L, RET_HEADS, RET_DV)).reshape(b, L, RET_V)
    y_ret = jax.nn.silu(g) * (y_ret * gn_gain)
    y_ssm = (ssm_ys[0] + ssm_ys[1]).reshape(b, L, SSM_D_INNER)
    y_ssm = rms_norm(y_ssm * jax.nn.silu(z)) * norm_gain
    out = jnp.concatenate([y_ret, y_ssm], axis=-1) @ w_out
    return out, jnp.stack(ret_fin, axis=1), jnp.stack(ssm_fin, axis=1)

def blocked_attention(q, k, v):
    b, L = q.shape[0], q.shape[1]
    nb = L // Q_BLOCK
    qb = jnp.moveaxis(q.reshape(b, nb, Q_BLOCK, ATT_KV_HEADS, ATT_RATIO, ATT_HD), 1, 0)
    scale = ATT_HD ** -0.5

    def one_block(qblk):
        s = jnp.einsum('bqgrd,bkgd->bgrqk', qblk, k, preferred_element_type=jnp.float32) * scale
        p = jax.nn.softmax(s, axis=-1)
        return jnp.einsum('bgrqk,bkgd->bqgrd', p.astype(v.dtype), v)

    o = lax.map(one_block, qb)
    return jnp.moveaxis(o, 0, 1).reshape(b, L, ATT_HEADS * ATT_HD)

def attention_mixer(h, kv_ctx, rope, w_qkv, q_gain, k_gain, w_o):
    b, L, _ = h.shape
    q, k, v = jnp.split(h @ w_qkv, [ATT_HEADS * ATT_HD, (ATT_HEADS + ATT_KV_HEADS) * ATT_HD], axis=-1)
    q = rms_norm(q.reshape(b, L, ATT_HEADS, ATT_HD)) * q_gain
    k = rms_norm(k.reshape(b, L, ATT_KV_HEADS, ATT_HD)) * k_gain
    v = v.reshape(b, L, ATT_KV_HEADS, ATT_HD)
    if rope is None:
        keys, vals = k, v
    else:
        q = apply_rope(q, rope[0], rope[1])
        keys = jnp.concatenate([kv_ctx[0], apply_rope(k, rope[0], rope[1])], axis=1)
        vals = jnp.concatenate([kv_ctx[1], v], axis=1)
    return blocked_attention(q, keys, vals) @ w_o, k, v

def conv_ffn(h, w_up, conv_w, conv_b, w_down):
    u = dwconv3(h @ w_up, conv_w, conv_b)
    a, val = jnp.split(u, 2, axis=-1)
    return (jax.nn.silu(a) * val) @ w_down

def trunk(x, cond, caches, P):
    b, L, _ = x.shape
    rope = None if caches is None else grid_rope_angles(L)
    ret_states, ssm_states, ks, vs = [], [], [], []
    for layer in range(DEPTH):
        mod = (jax.nn.silu(cond) @ P['w_mod'][layer] + P['b_mod'][layer])[:, None, :]
        sh1, sc1, g1, sh2, sc2, g2 = jnp.split(mod, 6, axis=-1)
        h = rms_norm(x) * P['norm_mix'][layer] * (1 + sc1) + sh1
        i = layer // 2
        if layer % 2 == 0:
            if caches is None:
                s_ret0 = jnp.zeros((b, 2, RET_HEADS, RET_DK, RET_DV), x.dtype)
                s_ssm0 = jnp.zeros((b, 2, SSM_HEADS, SSM_STATE, SSM_HEADDIM), x.dtype)
            else:
                s_ret0, s_ssm0 = caches[0][:, i], caches[1][:, i]
            y, s_ret, s_ssm = hybrid_mixer(
                h, s_ret0, s_ssm0, P['hyb_w_in'][i], P['hyb_w_out'][i], P['ret_log_decay'][i],
                P['ret_gn_gain'][i], P['ssm_conv_w'][i], P['ssm_conv_b'][i], P['ssm_a_log'][i],
                P['ssm_dt_bias'][i], P['ssm_d'][i], P['ssm_norm_gain'][i])
            ret_states.append(s_ret)
            ssm_states.append(s_ssm)
        else:
            kv_ctx = None if caches is None else (caches[2][:, i], caches[3][:, i])
            y, k_new, v_new = attention_mixer(h, kv_ctx, rope, P['attn_w_qkv'][i], P['attn_q_gain'][i],
                                              P['attn_k_gain'][i], P['attn_w_o'][i])
            ks.append(k_new)
            vs.append(v_new)
        x = x + g1 * y
        h = rms_norm(x) * P['norm_ffn'][layer] * (1 + sc2) + sh2
        x = x + g2 * conv_ffn(h, P['ffn_w_up'][layer], P['ffn_conv_w'][layer], P['ffn_conv_b'][layer],
                              P['ffn_w_down'][layer])
    return x, ret_states, ssm_states, ks, vs

def setup_inputs(seed: int = 0) -> dict:
    key = jax.random.key(seed)
    ks = iter(jax.random.split(key, 40))
    f32 = jnp.float32

    def nrm(shape, scale):
        return scale * jax.random.normal(next(ks), shape, f32)

    base_decay = jnp.log(1.0 - 2.0 ** (-5.0 - jnp.arange(RET_HEADS, dtype=f32)))
    ret_log_decay = base_decay * jnp.exp(nrm((N_EVEN, 2, RET_HEADS), 0.1))
    ssm_a_log = jnp.log(jax.random.uniform(next(ks), (N_EVEN, 2, SSM_HEADS), f32, 1.0, 16.0))
    dt0 = jnp.exp(jax.random.uniform(next(ks), (N_EVEN, 2, SSM_HEADS), f32, np.log(1e-3), np.log(1e-1)))
    ssm_dt_bias = dt0 + jnp.log(-jnp.expm1(-dt0))
    return {
        'x_prompt': nrm((BATCH, SEQ, D_MODEL), 1.0),
        'x_sample': nrm((DEC_BATCH, DEC_SEQ, D_MODEL), 1.0),
        'state_ret': nrm((DEC_BATCH, N_EVEN, 2, RET_HEADS, RET_DK, RET_DV), 0.5),
        'state_ssm': nrm((DEC_BATCH, N_EVEN, 2, SSM_HEADS, SSM_STATE, SSM_HEADDIM), 0.1),
        'cache_attn_k': nrm((DEC_BATCH, N_ODD, PAST_LEN, ATT_KV_HEADS, ATT_HD), 1.0),
        'cache_attn_v': nrm((DEC_BATCH, N_ODD, PAST_LEN, ATT_KV_HEADS, ATT_HD), 1.0),
        'c': nrm((DEC_BATCH, D_MODEL), 1.0),
        'c_ctx': nrm((D_MODEL,), 1.0),
        'w_mod': nrm((DEPTH, D_MODEL, 6 * D_MODEL), 0.5 * D_MODEL ** -0.5),
        'b_mod': nrm((DEPTH, 6 * D_MODEL), 0.02),
        'norm_mix': 1.0 + nrm((DEPTH, D_MODEL), 0.1),
        'norm_ffn': 1.0 + nrm((DEPTH, D_MODEL), 0.1),
        'ffn_w_up': nrm((DEPTH, D_MODEL, 2 * FFN_HIDDEN), D_MODEL ** -0.5),
        'ffn_conv_w': nrm((DEPTH, 3, 2 * FFN_HIDDEN), 3 ** -0.5),
        'ffn_conv_b': nrm((DEPTH, 2 * FFN_HIDDEN), 0.02),
        'ffn_w_down': nrm((DEPTH, FFN_HIDDEN, D_MODEL), FFN_HIDDEN ** -0.5),
        'hyb_w_in': nrm((N_EVEN, D_MODEL, HYB_IN), D_MODEL ** -0.5),
        'hyb_w_out': nrm((N_EVEN, HYB_MIX, D_MODEL), HYB_MIX ** -0.5),
        'ret_log_decay': ret_log_decay,
        'ret_gn_gain': 1.0 + nrm((N_EVEN, RET_V), 0.1),
        'ssm_conv_w': nrm((N_EVEN, 3, SSM_XBC), 3 ** -0.5),
        'ssm_conv_b': nrm((N_EVEN, SSM_XBC), 0.02),
        'ssm_a_log': ssm_a_log,
        'ssm_dt_bias': ssm_dt_bias,
        'ssm_d': 1.0 + nrm((N_EVEN, 2, SSM_HEADS), 0.1),
        'ssm_norm_gain': 1.0 + nrm((N_EVEN, SSM_D_INNER), 0.1),
        'attn_w_qkv': nrm((N_ODD, D_MODEL, ATT_QKV), D_MODEL ** -0.5),
        'attn_q_gain': 1.0 + nrm((N_ODD, ATT_HD), 0.1),
        'attn_k_gain': 1.0 + nrm((N_ODD, ATT_HD), 0.1),
        'attn_w_o': nrm((N_ODD, ATT_HEADS * ATT_HD, D_MODEL), (ATT_HEADS * ATT_HD) ** -0.5),
    }

def reference(x_prompt, x_sample, state_ret, state_ssm, cache_attn_k, cache_attn_v, c, c_ctx,
              w_mod, b_mod, norm_mix, norm_ffn, ffn_w_up, ffn_conv_w, ffn_conv_b, ffn_w_down,
              hyb_w_in, hyb_w_out, ret_log_decay, ret_gn_gain, ssm_conv_w, ssm_conv_b, ssm_a_log,
              ssm_dt_bias, ssm_d, ssm_norm_gain, attn_w_qkv, attn_q_gain, attn_k_gain, attn_w_o):
    P = {
        'w_mod': w_mod, 'b_mod': b_mod, 'norm_mix': norm_mix, 'norm_ffn': norm_ffn,
        'ffn_w_up': ffn_w_up, 'ffn_conv_w': ffn_conv_w, 'ffn_conv_b': ffn_conv_b, 'ffn_w_down': ffn_w_down,
        'hyb_w_in': hyb_w_in, 'hyb_w_out': hyb_w_out, 'ret_log_decay': ret_log_decay,
        'ret_gn_gain': ret_gn_gain, 'ssm_conv_w': ssm_conv_w, 'ssm_conv_b': ssm_conv_b,
        'ssm_a_log': ssm_a_log, 'ssm_dt_bias': ssm_dt_bias, 'ssm_d': ssm_d, 'ssm_norm_gain': ssm_norm_gain,
        'attn_w_qkv': attn_w_qkv, 'attn_q_gain': attn_q_gain, 'attn_k_gain': attn_k_gain, 'attn_w_o': attn_w_o,
    }
    y_prompt, rs, ss, ks, vs = trunk(x_prompt, c_ctx[None, :], None, P)
    new_state_ret = jnp.stack(rs, axis=1)
    new_state_ssm = jnp.stack(ss, axis=1)
    new_cache_attn_k = jnp.stack(ks, axis=1)
    new_cache_attn_v = jnp.stack(vs, axis=1)
    y_sample = trunk(x_sample, c, (state_ret, state_ssm, cache_attn_k, cache_attn_v), P)[0]
    return (y_prompt, y_sample, new_state_ret, new_state_ssm, new_cache_attn_k, new_cache_attn_v)


_drawn_inputs = setup_inputs


def setup_inputs(seed=0):
    import zlib

    import numpy as np

    out = dict(_drawn_inputs(seed))
    spreads = {}
    factors = {'state_ret': 3.338,
     'state_ssm': 4.038,
     'cache_attn_k': 8.0,
     'cache_attn_v': 7.116,
     'ffn_conv_b': 7.553,
     'ret_gn_gain': 3.933,
     'ssm_d': 6.561,
     'ssm_norm_gain': 2.669,
     'attn_q_gain': 8.0}
    for name, (base, spread) in spreads.items():
        noise = np.random.default_rng([zlib.crc32(name.encode()), seed]).standard_normal(out[name].shape)
        drawn = base * np.exp(spread * noise) if base else spread * noise
        out[name] = jnp.asarray(drawn.astype(out[name].dtype))
    for name, factor in factors.items():
        out[name] = (out[name] * factor).astype(out[name].dtype)
    return out
```

```python
import concourse.bass as bass
from concourse import mybir
from contextlib import ExitStack

D_MODEL, SEQ, DEC, PAST = 1024, 128, 512, 128
KT = D_MODEL // 128
FFN = 2816
FT = FFN // 128
PARTS = [8, 7, 7]
FIRST = [0, 8, 15]
NCH = 5
TOK = 644
HALF = TOK // 2
COL = [0, 130, 258, 386, 514]
PROMPT, SAMPLE = (0, 128), (130, 642)
EMPTY = (128, 642)
RH, RDK, RDV = 8, 64, 128
SH, SG, SR, SN, SP_ = 16, 4, 4, 128, 64
AH, AG, AR, AD = 16, 4, 4, 64
EPS = 1e-6
UNIT = 1024
RAW = 4

C_ID, C_TRIF, C_TRIB, C_NEGF, C_NEGB, C_IJF, C_IJB, C_ONES, C_ID2 = [128 * n for n in range(9)]
C_COMB = C_ID2 + 64
C_SIGN = C_COMB + 2
C_RPOS = C_SIGN + 1
C_EPS = C_RPOS + 4
C_ALL = C_EPS + 1


def constants():
    import numpy as np
    c = np.zeros((128, C_ALL), np.float32)
    j, i = np.meshgrid(np.arange(128), np.arange(128), indexing="ij")
    c[:, C_ID:C_ID + 128] = j == i
    c[:, C_TRIF:C_TRIF + 128] = j <= i
    c[:, C_TRIB:C_TRIB + 128] = j >= i
    c[:, C_NEGF:C_NEGF + 128] = np.where(j <= i, 0, -1e30)
    c[:, C_NEGB:C_NEGB + 128] = np.where(j >= i, 0, -1e30)
    c[:, C_IJF:C_IJF + 128] = np.maximum(i - j, 0)
    c[:, C_IJB:C_IJB + 128] = np.maximum(j - i, 0)
    c[:, C_ONES:C_ONES + 128] = 1
    c[:, C_ID2:C_ID2 + 64] = (np.arange(128)[:, None] % 64) == np.arange(64)[None]
    c[0:4, C_COMB:C_COMB + 2] = np.array([[1, 0], [0, 1], [1, 0], [0, 1]])
    for r in (0, 32):
        c[r:r + SH, C_SIGN] = 1
        c[64 + r:64 + r + SH, C_SIGN] = -1
    n = np.arange(128)
    for k, v in enumerate((n + 1, 128 - n, 127 - n, n)):
        c[:, C_RPOS + k] = v
    c[:, C_EPS] = EPS
    return c


def rope_tables():
    import numpy as np
    inv = np.float32(10000.0) ** (-np.arange(16, dtype=np.float32) / np.float32(16))
    t = np.arange(DEC)
    ang = np.stack([(t // 64).astype(np.float32)[:, None] * inv, (t % 64).astype(np.float32)[:, None] * inv], 1)
    cos = np.repeat(np.cos(ang)[:, :, None], 2, 2)
    sin = np.stack([-np.sin(ang), np.sin(ang)], 2)
    both = np.stack([cos, sin], 0).reshape(2, 4, 128, 64)
    return np.ascontiguousarray(both.transpose(2, 0, 1, 3)).astype(np.float32)


def build(nc, a, o, upto=None):
    F32, F32R = mybir.dt.float32, mybir.dt.float32r
    ACT, ALU, AX = mybir.ActivationFunctionType, mybir.AluOpType, mybir.AxisListType
    ds = bass.ds
    ADD, SUB, MUL, MAX, MIN = ALU.add, ALU.subtract, ALU.mult, ALU.max, ALU.min

    class Stage:
        pass

    stages, order = {}, []

    def stage(name, K, M, src, fm=True, whole=False):
        s = Stage()
        s.name, s.K, s.M, s.src, s.fm, s.whole = name, K, M, src, fm, whole
        s.u0 = sum(t.M for t in order)
        s.f0 = sum(t.M for t in order if t.fm)
        stages[name] = s
        order.append(s)

    hyb = a["hyb_in"]
    stage("modA", KT, 2 * KT, a["w_modA"], fm=False, whole=True)
    stage("dt", KT, 1, hyb[0:1])
    stage("xs", KT, 8, hyb[1:9])
    stage("bc", KT, 8, hyb[9:17])
    stage("z", KT, 8, hyb[17:25])
    stage("modB", KT, 96 - 2 * KT, a["w_modB"], fm=False)
    stage("qk", KT, 8, hyb[25:33])
    stage("v", KT, 8, hyb[33:41])
    stage("g", KT, 8, hyb[41:49])
    stage("wo_ssm", KT, 8, a["hyb_out"][1])
    stage("wo_ret", KT, 8, a["hyb_out"][0])

    def ffn_stages(l):
        for n, (first, K) in enumerate(zip(FIRST, PARTS)):
            stage(f"up{l}{n}", KT, 2 * K, a["ffn_up"][l, 2 * first:2 * (first + K)])
            stage(f"dn{l}{n}", K, 8, a["ffn_down"][l][:, :, first * 128:(first + K) * 128])

    ffn_stages(0)
    stage("qkv", KT, 12, a["qkv"])
    stage("wo", KT, 8, a["attn_o"])
    ffn_stages(1)
    KOF = [s.K for s in order for _ in range(s.M)]
    UNITS = len(KOF)
    WHOLE = [s.whole for s in order for _ in range(s.M)]
    SI = [sum(not m for m in WHOLE[:b]) for b in range(UNITS)]

    tp_base, tpf_base, n, full = {}, {}, 0, 0
    for name, uses in (("norm00", 1), ("xs", 8), ("b", 4), ("da", 1), ("cumT", 1), ("ssd", 12), ("again", 1),
                       ("k", 4), ("v", 8), ("normS", 1), ("retT", 8), ("norm01", 1),
                       ("norm10", 1), ("qkv", 12), ("qkT", 12), ("att", AG * NCH * AR), ("norm11", 1)):
        tp_base[name], tpf_base[name] = n, full
        n += uses
        full += uses

    ctx = ExitStack()
    with ctx:
        sems = {}

        def S(name):
            if name not in sems:
                sems[name] = ctx.enter_context(nc.semaphore(name))
            return sems[name]

        def sb(name, shape, dt=F32):
            return ctx.enter_context(nc.sbuf_tensor(name, shape, dt))

        cst = sb("cst", [128, C_ALL])
        ident = cst[:, C_ID:C_ID + 128]
        tri = [cst[:, C_TRIF:C_TRIF + 128], cst[:, C_TRIB:C_TRIB + 128]]
        ones = cst[:, C_ONES:C_ONES + 128]
        eps = cst[:, C_EPS:C_EPS + 1]
        x = sb("x", [128, KT, TOK])
        raw = sb("raw", [128, RAW, UNIT])
        w_hi, w_lo = sb("w_hi", [128, 2, UNIT], F32R), sb("w_lo", [128, 2, UNIT], F32R)
        cond, csil = sb("cond", [128, KT, 2]), sb("csil", [128, KT, 2])
        cond_r = sb("cond_r", [128, KT, 128], F32R)
        modrow = sb("modrow", [4, 2, 512])
        modT = sb("modT", [128, 2, 48, 2])
        bmod = sb("bmod", [128, 2, 48])
        norms = sb("norms", [128, 2, 2, KT])
        gains = sb("gains", [128, 2, 2, KT, 2])
        ssmgain, gngain = sb("ssmgain", [128, KT]), sb("gngain", [128, KT])
        fconv, sconv = sb("fconv", [128, 2, 2 * FT, 4]), sb("sconv", [128, 16, 4])
        ident_r = sb("ident_r", [128, 128], F32R)
        id2_r, nid2_r = sb("id2_r", [128, 64], F32R), sb("nid2_r", [128, 64], F32R)
        neg_r = sb("neg_r", [128, 2, 128], F32R)
        ssq, rs = sb("ssq", [128, TOK]), sb("rs", [128, 2, NCH])
        hf2 = sb("hf2", [128, 2, TOK])
        u_sb, t_sb = sb("u_sb", [128, 2, TOK]), sb("t_sb", [128, 2, TOK])
        sq, tn = u_sb, t_sb
        dtp = sb("dtp", [128, 3])
        lrow, lpair = sb("lrow", [128, 16]), sb("lpair", [128, 2, 4])
        drow, dsum = sb("drow", [128, 2, SH]), sb("dsum", [128, SH])
        qkgain = sb("qkgain", [128, 2, 64])

        H_BYTES = 2 * KT * TOK * 4
        h_hi, h_lo = sb("h_hi", [128, KT, TOK], F32R), sb("h_lo", [128, KT, TOK], F32R)
        H0 = nc.sbuf_base - H_BYTES
        A0 = nc.sbuf_base
        arena = sb("arena", [128, (nc.sbuf_bytes_remaining - 64) // 4])
        A_BYTES = (arena.shape[1]) * 4

        class Region:

            def __init__(self, at, size):
                self.at, self.end = at, at + size

            def __call__(self, name, shape, dt=F32):
                n = 4
                for k in shape[1:]:
                    n *= k
                n = -(-n // 32) * 32
                assert self.at + n <= self.end, (name, self.at + n - self.end)
                t = nc.alloc_sbuf_tensor_at(name, shape, dt, offset=self.at)
                self.at += n
                return t

        A = Region(A0, A_BYTES)
        zT = A("zT", [128, KT, TOK])
        mark = A.at
        bcT = A("bcT", [128, 8, TOK])
        xsTM = A("xsTM", [128, NCH, 1024])
        bTM = A("bTM", [128, NCH, 512])
        daT, da1, da2 = A("daT", [128, TOK]), A("da1", [128, TOK]), A("da2", [128, TOK])
        st_at = A.at
        sT = A("sT", [128, 2, TOK])
        daTM = A("daTM", [128, NCH, 128])
        B = Region(H0, H_BYTES)
        ecum, etot, wdt = B("ecum", [128, NCH, 64]), B("etot", [128, NCH, 64]), B("wdt", [128, NCH, 64])
        cum_r = B("cum_r", [128, NCH, 128], F32R)
        E = B("E", [128, 2, NCH, 128])
        GT = B("GT", [128, NCH, 128])
        xv = B("xv", [128, 2, 4, NCH, 64])
        Sst = B("Sst", [128, 2, 6, 64])
        s0 = B("s0", [128, 2, SH, 64])
        inter = B("inter", [128, 2, 4, 64])
        sout = A("sout", [128, 2, SH, 64])
        yb = Region(st_at, 2 * TOK * 4)("yb", [128, 2, NCH, 128])
        A = Region(mark, A0 + A_BYTES - mark)
        qkT = A("qkT", [128, 8, TOK])
        kTM, vTM = A("kTM", [128, NCH, 512]), A("vTM", [128, NCH, 1024])
        gT = A("gT", [128, KT, TOK])
        sT2 = u_sb
        yret = Region(A0, mark - A0)("yret", [128, NCH, 1024])
        B = Region(H0, H_BYTES)
        mTf, mTb = B("mTf", [128, RH, 128]), B("mTb", [128, RH, 128])
        PTr = B("PTr", [128, 2, NCH, 128])
        kw = B("kw", [128, 2, NCH, 128])
        Sr = B("Sr", [128, 4, 2, 128])
        s0r, soutr = B("s0r", [128, 4, 2, 128]), B("soutr", [128, 2, 4, 128])
        rdec = B("rdec", [128, 4, 16])
        rtot = B("rtot", [128, 2, 4])
        bst, mv, rsd = B("bst", [128, RH, NCH, 6]), B("mv", [128, RH, NCH, 2]), B("rsd", [128, RH, NCH])
        A = Region(A0, A_BYTES)
        qkv = A("qkv", [128, NCH, 1536])
        qT = A("qT", [128, KT, TOK])
        kT = A("kT", [128, AG, 6, 128])
        vpast = A("vpast", [128, 256])
        mark = A.at
        PT = A("PT", [128, 2, NCH, AR, 128])
        Pr = A("Pr", [128, 2, 640])
        amax, asum = A("amax", [128, 2, 4]), A("asum", [128, 2, 2])
        sT3 = Region(mark, 99999)("sT3", [128, 2, TOK])
        W = Region(mark, 99999)
        rt1, rt2 = W("rt1", [128, 1280]), W("rt2", [128, 1280])
        astat = W("astat", [128, 3, NCH, 20])
        rope = Region(H0, H_BYTES)("rope", [128, 2, 4, 64])
        A = Region(A0, A_BYTES)
        hid_hi, hid_lo = A("hid_hi", [128, 8, TOK], F32R), A("hid_lo", [128, 8, TOK], F32R)

        ps = ctx.enter_context(nc.psum_tensor("ps", [128, 8, 512], F32))

        def pj(f):
            return ps[:, 2 * (f % 2):2 * (f % 2) + 2, 0:HALF]

        flat = ps[:, :, :].rearrange("p b c -> p (b c)")
        TP = flat[:, 2048:2048 + 640].rearrange("p (c t) -> p c t", c=NCH)
        B6, B7 = flat[:, 3072:3584], flat[:, 3584:4096]

        def two(ap):
            return ap.rearrange("p (h c) -> p h c", h=2)

        def tile(t, k):
            return t[:, ds(k, 1), :].rearrange("p a c -> p (a c)")

        def chunk(c):
            return slice(COL[c], COL[c] + 128)

        def for_units(eng, s, body, step=4, peel=0, look=2):
            n = 0
            while step * (n + 1) <= s.M and all(
                s.u0 + step * n + r + look < UNITS and KOF[s.u0 + step * n + r + look] == s.K
                and not WHOLE[s.u0 + step * n + r + look] for r in range(step)
            ):
                n += 1
            if n < peel + 2:
                n = 0
            if n:
                for r in range(step * peel):
                    body(r, 0)
                with eng.Fori(peel, n) as j:
                    for r in range(step):
                        body(r, j)
            for r in range(step * n, s.M):
                body(r, 0)

        def sp_unit(sp, s, r, j):
            b = s.u0 + r
            if not isinstance(j, int) or j > 0:
                if not s.whole:
                    sp.wait_ge(S("w_lo"), SI[b] - 3 + 4 * j)
                else:
                    sp.wait_ge(S("pe_unit"), b - 3 + 4 * j)
            elif b >= RAW and WHOLE[b - RAW]:
                sp.wait_ge(S("pe_unit"), b - RAW + 1)
            elif b >= RAW:
                sp.wait_ge(S("w_lo"), SI[b - RAW] + 1)
            sp.dma_start(raw[:, b % RAW, 0:s.K * 128],
                         s.src[ds(r + 4 * j, 1)].rearrange("a p n -> (a p) n")).then_inc(S(f"w_in{b % RAW}"), 16)

        def act_split(act, b, j=0):
            if b >= UNITS or WHOLE[b]:
                return
            n, i = KOF[b] * 128, SI[b]
            if i >= 2:
                act.wait_ge(S("pe_unit"), b - 1 + 4 * j)
            act.wait_ge(S(f"w_in{b % RAW}"), 16 * (b // RAW + 1) + 16 * j)
            act.activation(w_hi[:, i % 2, 0:n], raw[:, b % RAW, 0:n], ACT.Copy).then_inc(S("w_hi"), 1)

        def dve_split(dve, b, j=0):
            if b >= UNITS or WHOLE[b]:
                return
            n, i = KOF[b] * 128, SI[b]
            dve.wait_ge(S("w_hi"), i + 1 + 4 * j)
            dve.tensor_tensor(w_lo[:, i % 2, 0:n], raw[:, b % RAW, 0:n], w_hi[:, i % 2, 0:n].bitcast(F32),
                              SUB).then_inc(S("w_lo"), 1)

        def pe_unit(pe, s, r, j, step, X, ready=None):
            i, f = SI[s.u0 + r], s.f0 + r
            pe.wait_ge(S("w_lo"), i + 1 + step * j)
            if f >= 2 or not isinstance(j, int):
                pe.wait_ge(S(f"pj_read{f % 2}"), f // 2 + (step // 2) * j)
            out = pj(f)
            for k in range(s.K):
                if ready:
                    pe.wait_ge(S(ready[0]), ready[1] + k + 1)
                ws = slice(k * 128, (k + 1) * 128)
                for n, (w, v) in enumerate(((w_hi, X[0]), (w_hi, X[1]), (w_lo, X[0]))):
                    for hh in range(2):
                        last = pe.matmul(out[:, hh, :], w[:, i % 2, ws], v[:, k, hh * HALF:(hh + 1) * HALF],
                                         start=(k == 0 and n == 0), stop=(k == s.K - 1 and n == 2))
            last.then_inc(S("pe_unit"), 1)

        def evac_wait(eng, s, r, j, step=4):
            eng.wait_ge(S("pe_unit"), s.u0 + r + 1 + step * j)

        def tp_read(s, r):
            return S(f"pj_read{(s.f0 + r) % 2}")

        def all_read(eng, f):
            for q in range(2):
                if (f + 1 - q) // 2:
                    eng.wait_ge(S(f"pj_read{q}"), (f + 1 - q) // 2)

        def tp_free(pe, t):
            pe.wait_ge(S("tp_read"), t)

        def tp_full(eng, t):
            eng.wait_ge(S("tp_full"), t + 1)

        H, HID = (h_hi, h_lo), (hid_hi, hid_lo)
        def pe_mod_unit(pe, s, r, j, out):
            b = s.u0 + r
            pe.wait_ge(S(f"w_in{b % RAW}"), 16 * (b // RAW + 1) + 16 * j)
            for k in range(KT):
                last = pe.matmul(out, raw[:, b % RAW, k * 128:(k + 1) * 128], csil[:, k, :],
                                 start=(k == 0), stop=(k == KT - 1))
            last.then_inc(S("pe_unit"), 1)

        def pe_modA(pe):
            s = stages["modA"]
            with pe.Fori(0, s.M // 4) as j:
                for r in range(4):
                    pe_mod_unit(pe, s, r, j, B6[:, ds(2 * r + 8 * j, 2)])

        ROWS = flat[:, 1536:2048]

        def pe_modB_unit(pe, m):
            s, q, r = stages["modB"], m // 4, m % 4
            i = SI[s.u0 + m]
            pe.wait_ge(S("w_lo"), i + 1)
            if r == 0 and q:
                pe.wait_ge(S("mod_rows"), q)
            for k in range(2):
                for n, w in enumerate((w_hi, w_lo)):
                    last = pe.matmul(ROWS, cond_r[:, 2 * r + k, :], w[:, i % 2, k * 512:(k + 1) * 512],
                                     start=(r + k + n == 0), stop=(r == 3 and k == 1 and n == 1))
            last.then_inc(S("pe_unit"), 1)

        def pe_modB_cols(pe, q):
            pe.wait_ge(S("mod_rows"), q + 1)
            for c in range(4):
                at = MODB + 8 * q + 2 * c
                last = pe.matmul(B7[:, at:at + 2], modrow[0:4, q % 5 % 2, c * 128:(c + 1) * 128],
                                 cst[0:4, C_COMB:C_COMB + 2], start=True, stop=True)
            last.then_inc(S("mod_cols"), 1)

        def act_modB(act, m, g):
            b, q = stages["modB"].u0 + m, m // 4
            act_split(act, b + 2, 5 * g)
            if m % 4 == 3:
                act.wait_ge(S("pe_unit"), b + 1 + 20 * g)
                if m >= 8:
                    act.wait_ge(S("mod_cols"), q - 1 + 5 * g)
                act.activation(modrow[:, q % 2, :], ROWS[0:4, :], ACT.Copy).then_inc(S("mod_rows"), 1)

        MODB = 320
        ALL_MODS = modT[:, :, :, :].rearrange("p l m g -> p (l m) g")
        ALL_BIAS = bmod[:, :, :].rearrange("p l m -> p (l m)")

        def dve_mod(dve, name, src):
            s = stages[name]
            t0, t1 = (0, s.M) if name == "modA" else (stages["modA"].M, 96)
            if name == "modA":
                dve.wait_ge(S("pe_unit"), s.u0 + s.M)
            else:
                dve.wait_ge(S("mod_cols"), 20)
            dve.tensor_tensor(ALL_MODS[:, t0:t1, :], src.rearrange("p (m g) -> p m g", g=2),
                              ALL_BIAS[:, t0:t1].unsqueeze(2).to_broadcast([128, t1 - t0, 2]), ADD).then_inc(S("mod"), 1)
            dve.wait_ge(S("mod"), 1 if name == "modA" else 3)
            for l, w in ((0, 0),) if name == "modA" else ((0, 1), (1, 0), (1, 1)):
                part = modT[:, l, (3 * w + 1) * KT:(3 * w + 2) * KT, :]
                ins = dve.scalar_tensor_tensor(gains[:, l, w, :, :], part, 1.0,
                                               norms[:, l, w, :].unsqueeze(2).to_broadcast([128, KT, 2]), ADD, MUL)
            ins.then_inc(S("mod"), 1)
            dve.wait_ge(S("mod"), 2 if name == "modA" else 4)

        def modcol(l, part, k, g):
            return modT[:, l, part * KT + k, g:g + 1]

        NORMS = ["norm00", "normS", "norm01", "norm10", "norm11"]
        APPLIED = ["norm00", "again", "normS", "retT", "norm01", "norm10", "norm11"]
        BY_RSTD = [p for p in APPLIED if p != "retT"]

        def act_square(act, name, k, src_k, ready=None):
            n = KT * NORMS.index(name) + k
            if ready:
                act.wait_ge(*ready)
            if n >= 2:
                act.wait_ge(S("sq_add"), n - 1)
            act.activation(sq[:, k % 2, :], src_k, ACT.Square).then_inc(S("sq"), 1)

        def dve_add_square(dve, name, k):
            n = KT * NORMS.index(name) + k
            dve.wait_ge(S("sq"), n + 1)
            if n:
                dve.wait_ge(S("sq_add"), n)
            if k == 0:
                dve.tensor_copy(ssq[:, :], sq[:, 0, :]).then_inc(S("sq_add"), 1)
            else:
                dve.tensor_tensor(ssq[:, :], ssq[:, :], sq[:, k % 2, :], ADD).then_inc(S("sq_add"), 1)

        MS = flat[:, 2048 + 640:2048 + 640 + NCH]

        def pe_norm(pe, name):
            pe.wait_ge(S("sq_add"), KT * (NORMS.index(name) + 1))
            tp_free(pe, tp_base[name])
            for c in range(NCH):
                last = pe.matmul(MS[:, c:c + 1], ssq[:, chunk(c)], ones[:, 0:1], start=True, stop=True)
            last.then_inc(S("ms"), 1)
            pe_spread(pe, name)

        def pe_spread(pe, name):
            pe.wait_ge(S("rstd"), 1 if name == "again" else NORMS.index(name) + 1)
            tp_free(pe, tp_base[name])
            for c in range(NCH):
                last = pe.matmul(TP[:, c, :], rs[:, 1, c:c + 1].to_broadcast([128, 128]), ident, start=True, stop=True)
            last.then_inc(S("tp_full"), 1)

        def act_root(act, name):
            act.wait_ge(S("ms"), NORMS.index(name) + 1)
            act.activation(rs[:, 0, :], MS, ACT.Sqrt, bias=eps, scale=1.0 / D_MODEL).then_inc(S("root"), 1)

        def dve_rstd(dve, name):
            dve.wait_ge(S("root"), NORMS.index(name) + 1)
            dve.reciprocal(rs[:, 1, :], rs[:, 0, :]).then_inc(S("rstd"), 1)

        GROUPS = ((PROMPT, 0), (SAMPLE, 128))

        def dve_apply(dve, name, src, scale, shift):
            n0, m0 = KT * APPLIED.index(name), KT * BY_RSTD.index(name)
            for h in H:
                for at in EMPTY:
                    dve.memset(h[:, :, at:at + 2].bitcast(F32), 0.0)
            tp_full(dve, tpf_base[name])
            for k in range(KT + 1):
                if k < KT:
                    if k == 0 and n0:
                        dve.wait_ge(S("h_hi"), n0)
                    if k >= 2:
                        dve.wait_ge(S("h_ready"), n0 + k - 1)
                    for g, ((c0, c1), at) in enumerate(GROUPS):
                        ins = dve.scalar_tensor_tensor(tn[:, k % 2, c0:c1], src[:, k, c0:c1], scale(k, g),
                                                       flat[:, 2048 + at:2048 + at + c1 - c0], MUL, MUL)
                    ins.then_inc(S("tn"), 1)
                if k:
                    dve.wait_ge(S("h_hi"), n0 + k)
                    for g, ((c0, c1), at) in enumerate(GROUPS):
                        hi = h_hi[:, k - 1, c0:c1].bitcast(F32)
                        if shift is None:
                            ins = dve.tensor_tensor(h_lo[:, k - 1, c0:c1], tn[:, (k - 1) % 2, c0:c1], hi, SUB)
                        else:
                            ins = dve.scalar_tensor_tensor(h_lo[:, k - 1, c0:c1], tn[:, (k - 1) % 2, c0:c1],
                                                           shift(k - 1, g), hi, ADD, SUB)
                    ins.then_inc(S("h_ready"), 1)
            dve.memset(ssq[:, 0:1], 0.0).then_inc(S("tp_read"), 1)

        def act_apply(act, name, shift=None):
            m0 = KT * BY_RSTD.index(name)
            for k in range(KT):
                act.wait_ge(S("tn"), m0 + k + 1)
                for g, ((c0, c1), at) in enumerate(GROUPS):
                    if shift is None:
                        ins = act.activation(h_hi[:, k, c0:c1], tn[:, k % 2, c0:c1], ACT.Copy)
                    else:
                        ins = act.activation(h_hi[:, k, c0:c1], tn[:, k % 2, c0:c1], ACT.Identity, bias=shift(k, g))
                ins.then_inc(S("h_hi"), 1)

        def hready(name):
            return ("h_ready", KT * APPLIED.index(name))

        def act_conv_in(act, s, r, j, cw):
            c = s.c0 + r
            if c >= 2:
                act.wait_ge(S("cv_done"), c - 1 + 4 * j)
            act.activation(two(u_sb[:, r % 2, :]), pj(s.f0 + r), ACT.Copy).then_inc(S("cv_u"), 1)
            act.activation(two(t_sb[:, r % 2, :]), pj(s.f0 + r), ACT.Identity, bias=cw[:, r + 4 * j, 3:4] if isinstance(j, int) else cw[:, ds(r + 4 * j, 1), 3],
                           scale=cw[:, r + 4 * j, 1:2] if isinstance(j, int) else cw[:, ds(r + 4 * j, 1), 1]).then_inc(tp_read(s, r), 1)

        def dve_conv(dve, s, r, j, cw):
            c, p, f = s.c0 + r, r % 2, s.f0 + r
            def w(n):
                return cw[:, r + 4 * j, n:n + 1] if isinstance(j, int) else cw[:, ds(r + 4 * j, 1), n]
            dve.wait_ge(tp_read(s, r), f // 2 + 1 + 2 * j)
            dve.scalar_tensor_tensor(t_sb[:, p, 1:TOK], u_sb[:, p, 0:TOK - 1], w(0), t_sb[:, p, 1:TOK],
                                     MUL, ADD).then_inc(S("cv_mid"), 1)
            dve.wait_ge(S("cv_mid"), c + 1 + 4 * j)
            dve.scalar_tensor_tensor(t_sb[:, p, 0:TOK - 1], u_sb[:, p, 1:TOK], w(2), t_sb[:, p, 0:TOK - 1],
                                     MUL, ADD).then_inc(S("cv_done"), 1)

        c = 0
        for name in ["xs", "bc"] + [f"up{l}{n}" for l in range(2) for n in range(3)]:
            stages[name].c0 = c
            c += stages[name].M
        c = 0
        for name in [f"up{l}{n}" for l in range(2) for n in range(3)]:
            stages[name].p0 = c
            c += stages[name].M // 2

        def pe_T(pe, name, i, src, ready):
            pe.wait_ge(*ready)
            tp_free(pe, tp_base[name] + i)
            for c in range(NCH):
                last = pe.transpose(TP[:, c, :], src[:, chunk(c)], ident)
            last.then_inc(S("tp_full"), 1)

        def dve_T(dve, name, i, dst):
            tp_full(dve, tpf_base[name] + i)
            dve.tensor_copy(dst, TP).then_inc(S("tp_read"), 1)

        PIECES = [(0, 0, 0, 128, 0), (1, 0, 130, HALF, 130), (1, 1, 0, 320, HALF)]

        def dve_residual(dve, s, r, gate):
            evac_wait(dve, s, r, 0)
            out = pj(s.f0 + r)
            for g, hh, a0, a1, c0 in PIECES:
                xs_ = x[:, r, c0:c0 + a1 - a0]
                ins = dve.scalar_tensor_tensor(xs_, out[:, hh, a0:a1], gate(r, g), xs_, MUL, ADD)
            ins.then_inc(tp_read(s, r), 1)

        def act_out_stage(act, s, norm=None):
            for r in range(s.M):
                evac_wait(act, s, r, 0)
                act_split(act, s.u0 + r + 2)
                if norm:
                    f = s.f0 + r
                    act_square(act, norm, r, x[:, r, :], (tp_read(s, r), f // 2 + 1))

        def dve_out_stage(dve, s, gate, norm=None):
            all_read(dve, s.f0)
            for r in range(s.M):
                dve_split(dve, s.u0 + r + 2)
                dve_residual(dve, s, r, gate)
                if norm and r:
                    dve_add_square(dve, norm, r - 1)
            if norm:
                dve_add_square(dve, norm, s.M - 1)

        def pe_stage(pe, s, X, ready=None, step=2):
            if ready:
                for r in range(2):
                    pe_unit(pe, s, r, 0, step, X, ready if r == 0 else None)
                if s.M % 2 == 0 and s.M > 4:
                    with pe.Fori(1, s.M // 2) as j:
                        for r in range(2):
                            pe_unit(pe, s, r, j, 2, X)
            else:
                with pe.Fori(0, s.M // 2) as j:
                    for r in range(2):
                        pe_unit(pe, s, r, j, 2, X)

        def act_up(act, s, l):
            cw = fconv[:, l, 2 * FIRST[s.part]:2 * (FIRST[s.part] + PARTS[s.part]), :]

            def body(r, j):
                evac_wait(act, s, r, j)
                act_split(act, s.u0 + r + 2, j)
                p = s.p0 + r // 2
                act_conv_in(act, s, r, j, cw)
                if r % 2:
                    act.wait_ge(S("cv_done"), s.c0 + r + 4 * j)
                    act.activation(t_sb[:, 0, :], t_sb[:, 0, :], ACT.Silu).then_inc(S("hid_silu"), 1)
                    act.wait_ge(S("hid_mul"), p + 1 + 2 * j)
                    act.activation(tile(hid_hi, r // 2 + 2 * j), hf2[:, 0, :], ACT.Copy).then_inc(S("hid_hi"), 1)

            for_units(act, s, body)

        def dve_up(dve, s, l):
            cw = fconv[:, l, 2 * FIRST[s.part]:2 * (FIRST[s.part] + PARTS[s.part]), :]

            def body(r, j):
                dve_split(dve, s.u0 + r + 2, j)
                dve_conv(dve, s, r, j, cw)
                if r % 2:
                    p = s.p0 + r // 2
                    dve.wait_ge(S("hid_silu"), p + 1 + 2 * j)
                    dve.wait_ge(S("cv_done"), s.c0 + r + 1 + 4 * j)
                    dve.tensor_tensor(hf2[:, 0, :], t_sb[:, 0, :], t_sb[:, 1, :], MUL).then_inc(S("hid_mul"), 1)
                    dve.wait_ge(S("hid_hi"), p + 1 + 2 * j)
                    dve.tensor_tensor(tile(hid_lo, r // 2 + 2 * j), hf2[:, 0, :],
                                      tile(hid_hi, r // 2 + 2 * j).bitcast(F32), SUB).then_inc(S("hid_ready"), 1)

            for_units(dve, s, body)

        for l in range(2):
            for n in range(3):
                stages[f"up{l}{n}"].part = n

        def dve_setup(dve):
            dve.wait_ge(S("ld_cst"), 16)
            dve.tensor_copy(ident_r[:, :], ident).then_inc(S("set"), 1)
            dve.tensor_copy(id2_r[:, :], cst[:, C_ID2:C_ID2 + 64]).then_inc(S("set"), 1)
            dve.tensor_scalar(nid2_r[:, :], cst[:, C_ID2:C_ID2 + 64], -1.0, None, MUL).then_inc(S("set"), 1)
            dve.tensor_copy(neg_r[:, :, :], cst[:, C_NEGF:C_NEGF + 256].rearrange("p (d c) -> p d c", d=2)).then_inc(S("set"), 1)
            dve.memset(cond_r[:, :, :].bitcast(F32), 0.0).then_inc(S("cond"), 1)
            dve.wait_ge(S("csil"), 1)
            dve.wait_ge(S("cond"), 1)
            dve.tensor_copy(cond_r[:, :, 0:2], csil[:, :, :]).then_inc(S("cond"), 1)
            dve.wait_ge(S("cond"), 2)
            dve.tensor_tensor(cond_r[:, :, 2:4], csil[:, :, :], cond_r[:, :, 0:2].bitcast(F32), SUB).then_inc(S("cond"), 1)

        def dve_small(dve):
            dve.wait_ge(S("ld_small"), 16 * N_SMALL)
            dve.wait_ge(S("dtp"), 1)
            dve.tensor_tensor(dtp[:, 2:3], dtp[:, 1:2], cst[:, C_SIGN:C_SIGN + 1], MUL).then_inc(S("set"), 1)
            dve.tensor_tensor(dsum[:, :], drow[:, 0, :], drow[:, 1, :], ADD).then_inc(S("set"), 1)

        def act_dt(act):
            s = stages["dt"]
            evac_wait(act, s, 0, 0)
            act_split(act, s.u0 + 2)
            act.wait_ge(S("ld_small"), 16 * N_SMALL)
            act.activation(two(da1[:, :]), pj(s.f0), ACT.Identity, bias=dtp[:, 0:1]).then_inc(tp_read(s, 0), 1)
            act.wait_ge(S("da"), 1)
            act.activation(da2[:, :], da2[:, :], ACT.Exp).then_inc(S("da_e"), 1)
            act.wait_ge(S("da_e"), 1)
            act.activation(sT[:, 0, :], da2[:, :], ACT.Ln, bias=1.0).then_inc(S("da_e"), 1)

        def dve_dt(dve):
            s = stages["dt"]
            dve_split(dve, s.u0 + 2)
            n = [0]

            def step(ins):
                n[0] += 1
                ins.then_inc(S("da"), 1)
                dve.wait_ge(S("da"), n[0])

            dve.wait_ge(tp_read(s, 0), s.f0 // 2 + 1)
            step(dve.scalar_tensor_tensor(da2[:, :], da1[:, :], -1.0, da1[:, :], MUL, MIN))
            step(dve.tensor_scalar(da1[:, :], da1[:, :], 0.0, None, MAX))
            dve.wait_ge(S("da_e"), 2)
            step(dve.tensor_scalar(sT[:, 1, :], da2[:, :], 1.0, None, ADD))
            step(dve.scalar_tensor_tensor(sT[:, 1, :], sT[:, 1, :], -1.0, da2[:, :], ADD, SUB))
            step(dve.tensor_tensor(da1[:, :], da1[:, :], sT[:, 0, :], ADD))
            step(dve.tensor_tensor(da1[:, :], da1[:, :], sT[:, 1, :], SUB))
            dve.wait_ge(S("set"), 6)
            step(dve.tensor_scalar(daT[:, :], da1[:, :], dtp[:, 2:3], None, MUL))
            assert n[0] == 7

        def pe_ssd_in(pe):
            xs_, bc, z = stages["xs"], stages["bc"], stages["z"]
            for r in range(2):
                pe_unit(pe, xs_, r, 0, 2, H)
            with pe.Fori(1, 4) as j:
                for r in range(2):
                    pe_unit(pe, xs_, r, j, 2, H)
                    pe_T(pe, "xs", r - 2 + 2 * j, sT[:, r, :], (S("silu"), r - 1 + 2 * j))
            for r in range(2):
                pe_unit(pe, bc, r, 0, 2, H)
                pe_T(pe, "xs", 6 + r, sT[:, r, :], (S("silu"), 7 + r))
            for r in range(4):
                pe_unit(pe, bc, 2 + r, 0, 2, H)
                pe_T(pe, "b", r, bcT[:, r, :], (S("silu"), 9 + r))
            for r in range(6, 8):
                pe_unit(pe, bc, r, 0, 2, H)
            pe_stage(pe, z, H)

        def act_ssd_in(act):
            for name in ("xs", "bc"):
                s = stages[name]
                for r in range(8):
                    c = s.c0 + r
                    evac_wait(act, s, r, 0)
                    act_split(act, s.u0 + r + 2)
                    act_conv_in(act, s, r, 0, sconv[:, c - r:c - r + 8, :])
                    if name == "xs":
                        if r >= 2:
                            act.wait_ge(S("tp_full"), tpf_base["xs"] + r - 1)
                        dst = sT[:, r % 2, :]
                    else:
                        dst = bcT[:, r, :]
                    act.wait_ge(S("cv_done"), c + 1)
                    act.activation(dst, t_sb[:, r % 2, :], ACT.Silu).then_inc(S("silu"), 1)
            s = stages["z"]
            for r in range(8):
                evac_wait(act, s, r, 0)
                act_split(act, s.u0 + r + 2)
                act.activation(two(zT[:, r, :]), pj(s.f0 + r), ACT.Silu).then_inc(tp_read(s, r), 1)

        def dve_ssd_in(dve):
            for name in ("xs", "bc"):
                s = stages[name]
                for r in range(8):
                    dve_split(dve, s.u0 + r + 2)
                    dve_conv(dve, s, r, 0, sconv[:, s.c0:s.c0 + 8, :])
                    i = s.c0 + r - 2
                    if 0 <= i < 8:
                        dve_T(dve, "xs", i, xsTM[:, :, i * 128:(i + 1) * 128])
                    elif 8 <= i < 12:
                        dve_T(dve, "b", i - 8, bTM[:, :, (i - 8) * 128:(i - 7) * 128])
            s = stages["z"]
            for r in range(8):
                dve_split(dve, s.u0 + r + 2)

        def pe_cum(pe):
            pe.wait_ge(S("da"), 7)
            pe_T(pe, "da", 0, daT[:, :], (S("da"), 7))
            pe.wait_ge(S("tp_read"), tp_base["da"] + 1)
            for c in range(NCH):
                for d in range(2):
                    pe.matmul(B6[:, c * 64 + d * 32:c * 64 + d * 32 + 32], tri[d],
                              daTM[:, c, 64 + 32 * d:96 + 32 * d], start=True, stop=True)
            pe.matmul(B7[:, 0:NCH * 64].rearrange("p (c h) -> p c h", c=NCH), ones, daTM[:, :, 64:128],
                      start=True, stop=True).then_inc(S("cum"), 1)
            tp_free(pe, tp_base["cumT"])
            for c in range(NCH):
                for d in range(2):
                    last = pe.matmul(TP[32 * d:32 * d + 32, c, :], daTM[:, c, 64 + 32 * d:96 + 32 * d], tri[d],
                                     start=True, stop=True)
            last.then_inc(S("tp_full"), 1)

        def act_cum(act):
            act.wait_ge(S("cum"), 1)
            all_read(act, stages["z"].f0 + 8)
            act.activation(ecum[:, :, :], B6[:, 0:320].rearrange("p (c h) -> p c h", c=NCH), ACT.Exp).then_inc(S("cum_e"), 1)
            act.activation(etot[:, :, :], B7[:, 0:320].rearrange("p (c h) -> p c h", c=NCH), ACT.Exp).then_inc(S("cum_e"), 1)
            act.wait_ge(S("cum_d"), 1)
            act.activation(wdt[:, :, :], wdt[:, :, :], ACT.Exp).then_inc(S("cum_e"), 1)
            tp_full(act, tpf_base["cumT"])
            act.activation(cum_r[0:64, :, :], TP[0:64, :, :], ACT.Copy).then_inc(S("cum_e"), 1)

        def dve_cum(dve):
            dve_T(dve, "da", 0, daTM[:, :, :])
            dve.wait_ge(S("cum_e"), 2)
            dve.tensor_copy(wdt[:, :, :], B7[:, 0:320].rearrange("p (c h) -> p c h", c=NCH)).then_inc(S("cum_c"), 1)
            dve.wait_ge(S("cum_c"), 1)
            dve.tensor_tensor(wdt[:, :, :], wdt[:, :, :], B6[:, 0:320].rearrange("p (c h) -> p c h", c=NCH),
                              SUB).then_inc(S("cum_d"), 1)
            dve.wait_ge(S("cum_e"), 4)
            dve.tensor_tensor(wdt[:, :, :], wdt[:, :, :], daTM[:, :, 0:64], MUL).then_inc(S("cum_d"), 1)
            dve.tensor_tensor(cum_r[64:128, :, :], TP[0:64, :, :], cum_r[0:64, :, :].bitcast(F32), SUB).then_inc(S("tp_read"), 1)

        INTO = {(0, 2): 0, (0, 3): 1, (0, 4): 2, (1, 3): 3, (1, 2): 4, (1, 1): 5}
        KV = [(0, 0), (1, 0), (0, 1), (0, 2), (0, 3), (1, 4), (1, 3), (1, 2)]

        def pe_ssd(pe):
            t0 = tp_base["ssd"]
            all_read(pe, stages["z"].f0 + 8)
            pe.wait_ge(S("tp_read"), t0)
            pe.wait_ge(S("cum_e"), 4)
            pe.wait_ge(S("cum_d"), 2)
            pe.wait_ge(S("set"), 4)
            pe.wait_ge(S("cond"), 3)

            def D(g, r):
                pe.wait_ge(S("ssd_E"), 2 * (4 * g + r))
                for d in range(2):
                    row = 32 * d + 4 * g + r
                    sel = id2_r[:, row:row + 1].to_broadcast([128, 128])
                    nsel = nid2_r[:, row:row + 1].to_broadcast([128, 128])
                    for c0, c1, at in ((0, 4, 512 * d), (4, 5, 1024 + 128 * d)):
                        out = flat[:, at:at + 128 * (c1 - c0)].rearrange("p (c t) -> p c t", t=128)
                        pe.matmul(out, sel, cum_r[:, c0:c1, :], start=True, stop=False)
                        pe.matmul(out, ident_r[:, :], neg_r[:, d:d + 1, :].to_broadcast([128, c1 - c0, 128]),
                                  start=False, stop=False)
                        for c in range(c0, c1):
                            last = pe.matmul(out[:, c - c0, :], cum_r[:, c, :], nsel, start=False, stop=(c == c1 - 1))
                last.then_inc(S("ssd_D"), 1)

            cols = list(range(20))

            def some_cols(m):
                while cols and 4 * cols[0] + 3 < m:
                    pe_modB_cols(pe, cols.pop(0))

            def group(g):
                tp_free(pe, t0 + 3 * g)
                for c in range(NCH):
                    last = pe.matmul(TP[:, c, :], tile(bcT, g)[:, chunk(c)], tile(bcT, SG + g)[:, chunk(c)],
                                     start=True, stop=True)
                last.then_inc(S("tp_full"), 1)
                D(g, 0)
                for r in range(SR):
                    h = 4 * g + r
                    if r < SR - 1:
                        D(g, r + 1)
                    for n in range(2):
                        pe_modB_unit(pe, 5 * h + n)
                    pe.wait_ge(S("ssd_in"), h)
                    pe.wait_ge(S("ssd_v"), 4 * h + 4)
                    for n, (d, c) in enumerate(KV):
                        last = pe.matmul(B6[:, n * 64:(n + 1) * 64], bTM[:, c, ds(g * 128, 128)], xv[:, r % 2, 2 + d, c, :],
                                         start=True, stop=True)
                    last.then_inc(S("ssd_kv"), 1)
                    pe_modB_unit(pe, 5 * h + 2)
                    pe.wait_ge(S("ssd_pt"), 2 * h + 2)
                    pe.wait_ge(S("ssd_yr"), h)
                    some_cols(5 * h)
                    for c in range(NCH):
                        for d in range(2):
                            last = pe.matmul(B7[:, c * 64:(c + 1) * 64], E[:, d, c, :], xv[:, r % 2, d, c, :],
                                             start=(d == 0), stop=(d == 1))
                    last.then_inc(S("ssd_y"), 1)
                    pe_modB_unit(pe, 5 * h + 3)
                    pe.wait_ge(S("ssd_rec"), 6 * h + 6)
                    for d in range(2):
                        for c in range(1, NCH):
                            st = Sst[:, r % 2, INTO[d, c], :] if (d, c) in INTO else \
                                s0[:, d, h, :]
                            last = pe.matmul(B6[:, (d * 4 + c - 1) * 64:(d * 4 + c) * 64],
                                             tile(bcT, SG + g)[:, chunk(c)], st, start=True, stop=True)
                    last.then_inc(S("ssd_i"), 1)
                    pe_modB_unit(pe, 5 * h + 4)
                    if r % 2:
                        q = r // 2
                        pe.wait_ge(S("ssd_yt"), h + 1)
                        tp_free(pe, t0 + 3 * g + 1 + q)
                        for c in range(NCH):
                            last = pe.transpose(TP[:, c, :], yb[:, q, c, :], ident)
                        last.then_inc(S("tp_full"), 1)

            for g in range(SG):
                group(g)
                pe.wait_ge(S("ssd_yr"), 4 * g + 4)
                some_cols(20 * g + 20)

        def act_ssd(act):
            t0, f0 = tp_base["ssd"], tpf_base["ssd"]
            with act.Fori(0, SG) as g:
                tp_full(act, f0 + 3 * g)
                act.activation(GT[:, :, :], TP, ACT.Copy).then_inc(S("tp_read"), 1)
                for r in range(SR):
                    h = 4 * g + r
                    act.wait_ge(S("ssd_D"), h + 1)
                    if r:
                        act.wait_ge(S("ssd_y"), h)
                    act.activation(E[:, :, 0:4, :].rearrange("p d c t -> p d (c t)"),
                                   flat[:, 0:1024].rearrange("p (d c) -> p d c", d=2), ACT.Exp).then_inc(S("ssd_E"), 1)
                    act.activation(E[:, :, 4, :], flat[:, 1024:1280].rearrange("p (d c) -> p d c", d=2),
                                   ACT.Exp).then_inc(S("ssd_E"), 1)
                    for n in range(5):
                        act_modB(act, 5 * r + n, g)

        def dve_ssd(dve):
            t0, f0 = tp_base["ssd"], tpf_base["ssd"]
            dve.wait_ge(S("ld_s0"), 16)
            dve.wait_ge(S("cum_d"), 2)
            with dve.Fori(0, SG) as g:
                for r in range(SR):
                    h = 4 * g + r

                    def mod(n):
                        dve_split(dve, stages["modB"].u0 + 5 * r + n + 2, 5 * g)

                    def row(t, d, c0=0, c1=NCH, w=64):
                        return t[:, c0:c1, ds(4 * g + r + 32 * d, 1)].to_broadcast([128, c1 - c0, w])

                    xh = xsTM[:, :, ds(h * 64, 64)]
                    if r >= 2:
                        dve.wait_ge(S("ssd_i"), h - 1)
                    for k, (t, d) in enumerate(((daTM, 0), (daTM, 1), (wdt, 0), (wdt, 1))):
                        dve.tensor_tensor(xv[:, r % 2, k, :, :], xh, row(t, d), MUL).then_inc(S("ssd_v"), 1)
                    mod(0)
                    dve.wait_ge(S("ssd_E"), 2 * h + 2)
                    for d in range(2):
                        dve.tensor_tensor(E[:, d, :, :], E[:, d, :, :], GT[:, :, :], MUL).then_inc(S("ssd_pt"), 1)
                    mod(1)
                    dve.wait_ge(S("ssd_kv"), h + 1)
                    dve.tensor_copy(sout[:, :, ds(h, 1), :].rearrange("p d a c -> p d (a c)"),
                                    B6[:, 0:128].rearrange("p (d c) -> p d c", d=2)).then_inc(S("ssd_so"), 1)
                    for k in range(3):
                        for d in range(2):
                            c = k + 1 if d == 0 else 4 - k
                            prev = s0[:, d, ds(h, 1), :].rearrange("p a c -> p (a c)") if k == 0 else \
                                Sst[:, r % 2, 3 * d + k - 1, :]
                            if k:
                                dve.wait_ge(S("ssd_rec"), 6 * h + 2 * k + d - 1)
                            ins = dve.scalar_tensor_tensor(
                                Sst[:, r % 2, 3 * d + k, :], prev, etot[:, c, ds(4 * g + r + 32 * d, 1)],
                                B6[:, (2 + 3 * d + k) * 64:(3 + 3 * d + k) * 64], MUL, ADD)
                            ins.then_inc(S("ssd_rec"), 1)
                    mod(2)
                    yh = yb[:, r // 2, :, (r % 2) * 64:(r % 2) * 64 + 64]
                    dve.wait_ge(S("ssd_y"), h + 1)
                    if r % 2 == 0:
                        dve.wait_ge(S("tp_full"), f0 + 3 * g)
                    dve.scalar_tensor_tensor(yh, xh, dsum[:, ds(h, 1)], B7[:, 0:320].rearrange("p (c v) -> p c v", c=NCH),
                                             MUL, ADD).then_inc(S("ssd_yr"), 1)
                    mod(3)
                    dve.wait_ge(S("ssd_i"), h + 1)
                    for d in range(2):
                        ins = dve.tensor_tensor(inter[:, d, :, :], B6[:, d * 256:(d + 1) * 256].rearrange("p (c v) -> p c v", c=4),
                                                row(ecum, d, 1, 5), MUL)
                    ins.then_inc(S("ssd_in"), 1)
                    dve.wait_ge(S("ssd_yr"), h + 1)
                    dve.wait_ge(S("ssd_in"), h + 1)
                    dve.tensor_tensor(yh[:, 1:5, :], yh[:, 1:5, :], inter[:, 0, :, :], ADD).then_inc(S("ssd_ya"), 1)
                    dve.wait_ge(S("ssd_ya"), h + 1)
                    dve.tensor_tensor(yh[:, 1:5, :], yh[:, 1:5, :], inter[:, 1, :, :], ADD).then_inc(S("ssd_yt"), 1)
                    mod(4)
                    if r % 2:
                        q = r // 2
                        tp_full(dve, f0 + 3 * g + 1 + q)
                        zt = zT[:, ds(2 * g + q, 1), :].rearrange("p a c -> p (a c)")
                        dve.tensor_tensor(zt[:, 0:128], zt[:, 0:128], TP[:, 0, :], MUL)
                        zs = zt[:, 130:642].rearrange("p (c t) -> p c t", c=4)
                        dve.tensor_tensor(zs, zs, TP[:, 1:5, :], MUL).then_inc(S("tp_read"), 1)

        def pe_ret_in(pe):
            qk, v, g_ = stages["qk"], stages["v"], stages["g"]
            for r in range(4):
                pe_unit(pe, qk, r, 0, 2, H, hready("again") if r == 0 else None)
            for r in range(4, 6):
                pe_unit(pe, qk, r, 0, 2, H)
            for r in range(6, 8):
                pe_unit(pe, qk, r, 0, 2, H)
                f = qk.f0 + r - 2
                pe_T(pe, "k", r - 6, qkT[:, r - 2, :], (S(f"pj_read{f % 2}"), f // 2 + 1))
            for r in range(2):
                pe_unit(pe, v, r, 0, 2, H)
                f = qk.f0 + 6 + r
                pe_T(pe, "k", 2 + r, qkT[:, 6 + r, :], (S(f"pj_read{f % 2}"), f // 2 + 1))
            with pe.Fori(1, 4) as j:
                for r in range(2):
                    pe_unit(pe, v, r, j, 2, H)
                    f = v.f0 + r
                    pe_T(pe, "v", r - 2 + 2 * j, sT2[:, r, :], (S(f"pj_read{f % 2}"), f // 2 + j))
            for r in range(2):
                pe_unit(pe, g_, r, 0, 2, H)
                f = v.f0 + 6 + r
                pe_T(pe, "v", 6 + r, sT2[:, r, :], (S(f"pj_read{f % 2}"), f // 2 + 1))
            with pe.Fori(1, 4) as j:
                for r in range(2):
                    pe_unit(pe, g_, r, j, 2, H)

        def act_ret_in(act):
            for name in ("qk", "v", "g"):
                s = stages[name]
                for r in range(8):
                    evac_wait(act, s, r, 0)
                    act_split(act, s.u0 + r + 2)
                    src = pj(s.f0 + r)
                    if name == "qk":
                        ins = act.activation(two(qkT[:, r, :]), src, ACT.Copy, scale=RDK ** -0.5 if r >= 4 else 1.0)
                    elif name == "v":
                        if r >= 2:
                            act.wait_ge(S("tp_full"), tpf_base["v"] + r - 1)
                        ins = act.activation(two(sT2[:, r % 2, :]), src, ACT.Copy)
                    else:
                        ins = act.activation(two(gT[:, r, :]), src, ACT.Silu)
                    ins.then_inc(tp_read(s, r), 1)

        def dve_ret_in(dve):
            for n, name in enumerate(("qk", "v", "g")):
                s = stages[name]
                for r in range(8):
                    dve_split(dve, s.u0 + r + 2)
                    i = 8 * n + r - 6
                    if 0 <= i < 4:
                        dve_T(dve, "k", i, kTM[:, :, i * 128:(i + 1) * 128])
                    elif 4 <= i < 12:
                        dve_T(dve, "v", i - 4, vTM[:, :, (i - 4) * 128:(i - 3) * 128])

        def act_ret_setup(act):
            act.wait_ge(S("pe_unit"), stages["wo_ssm"].u0 + 8)
            for d, (m, at) in enumerate(((mTf, C_IJF), (mTb, C_IJB))):
                for h in range(RH):
                    last = act.activation(m[:, h, :], cst[:, at:at + 128], ACT.Exp, scale=lrow[:, d * 8 + h:d * 8 + h + 1])
            last.then_inc(S("ret_set"), 1)
            for n in range(4):
                last = act.activation(rdec[:, n, :], lrow[:, :], ACT.Exp, scale=cst[:, C_RPOS + n:C_RPOS + n + 1])
            act.activation(rtot[:, :, :], lpair[:, :, :], ACT.Exp, scale=128.0).then_inc(S("ret_set"), 1)

        def dve_ret_setup(dve):
            dve.wait_ge(S("ret_set"), 1)
            for d, m in enumerate((mTf, mTb)):
                dve.tensor_tensor(m[:, :, :], m[:, :, :], tri[d].unsqueeze(1).to_broadcast([128, RH, 128]),
                                  MUL).then_inc(S("ret_m"), 1)
            dve.wait_ge(S("ret_m"), 2)
            dve.tensor_tensor(mTf[:, :, :], mTf[:, :, :], mTb[:, :, :], ADD).then_inc(S("ret_m"), 1)

        def pe_ret(pe):
            all_read(pe, stages["wo_ssm"].f0 + 8)
            pe.wait_ge(S("tp_read"), tp_base["normS"] + 1)
            for p in range(4):
                if p:
                    pe.wait_ge(S("ret_rd"), 4 * p)
                for e in range(2):
                    rows = slice(64 * e, 64 * e + 64)
                    out = flat[:, 1024 * e:1024 * e + 640].rearrange("p (c t) -> p c t", c=NCH)
                    for c in range(NCH):
                        last = pe.matmul(out[:, c, :], tile(qkT, 4 + p)[rows, chunk(c)], tile(qkT, p)[rows, chunk(c)],
                                         start=True, stop=True)
                    last.then_inc(S("ret_s"), 1)
                pe.wait_ge(S("ret_kw"), 4 * p + 4)
                for n, (d, c) in enumerate(KV):
                    for e in range(2):
                        last = pe.matmul(flat[64 * e:64 * e + 64, 2048 + n * 128:2048 + (n + 1) * 128],
                                         kw[:, d, c, 64 * e:64 * e + 64], vTM[:, c, ds(p * 256 + 128 * e, 128)],
                                         start=True, stop=True)
                last.then_inc(S("ret_kv"), 1)
                for e in range(2):
                    rows = slice(64 * e, 64 * e + 64)
                    pe.wait_ge(S("ret_pt"), 2 * p + e + 1)
                    out = flat[:, 1024 * e:1024 * e + 640].rearrange("p (c t) -> p c t", c=NCH)
                    for c in range(NCH):
                        last = pe.matmul(out[:, c, :], PTr[:, e, c, :], vTM[:, c, ds(p * 256 + 128 * e, 128)],
                                         start=True, stop=True)
                    last.then_inc(S("ret_y"), 1)
                    if e == 0:
                        pe.wait_ge(S("ret_rec"), 8 * p + 8)
                    else:
                        pe.wait_ge(S("ret_rd"), 4 * p + 2)
                    for c in range(1, NCH):
                        last = pe.matmul(flat[:, 3072 + (c - 1) * 256:3072 + c * 256], tile(qkT, p)[rows, chunk(c)],
                                         Sr[rows, c - 1, :, :].rearrange("p d v -> p (d v)"), start=True, stop=True)
                    last.then_inc(S("ret_i"), 1)

        def act_ret(act):
            act.wait_ge(S("tp_read"), tp_base["v"] + 8)
            act.wait_ge(S("ret_set"), 2)
            act.wait_ge(S("h_ready"), KT * (APPLIED.index("normS") + 1))
            with act.Fori(0, 4) as p:
                for d in range(2):
                    for e in range(2):
                        act.activation(kw[:, d, :, 64 * e:64 * e + 64], kTM[:, :, ds(p * 128 + 64 * e, 64)], ACT.Copy,
                                       scale=rdec[:, 2 + d, ds(2 * p + e + 8 * d, 1)]).then_inc(S("ret_kw"), 1)
                for e in range(2):
                    act.wait_ge(S("ret_y"), 2 * p + e + 1)
                    act.activation(yret[:, :, ds(p * 256 + e * 128, 128)],
                                   flat[:, 1024 * e:1024 * e + 640].rearrange("p (c t) -> p c t", c=NCH),
                                   ACT.Copy).then_inc(S("ret_yc"), 1)

        def dve_ret(dve):
            dve.wait_ge(S("ret_m"), 3)
            dve.wait_ge(S("ld_s0r"), 16)
            with dve.Fori(0, 4) as p:
                for e in range(2):
                    dve.wait_ge(S("ret_s"), 2 * p + e + 1)
                    dve.tensor_tensor(PTr[:, e, :, :], flat[:, 1024 * e:1024 * e + 640].rearrange("p (c t) -> p c t", c=NCH),
                                      mTf[:, ds(2 * p + e, 1), :].to_broadcast([128, NCH, 128]), MUL).then_inc(S("ret_pt"), 1)
                dve.wait_ge(S("ret_kv"), p + 1)
                kv = flat[:, 2048:3072].rearrange("p (n v) -> p n v", n=8)
                dve.tensor_copy(soutr[:, :, ds(p, 1), :].rearrange("p d a v -> p d (a v)"), kv[:, 0:2, :]).then_inc(S("ret_so"), 1)
                for d in range(2):
                    dve.tensor_copy(Sr[:, 3 * d, d, :], s0r[:, ds(p, 1), d, :].rearrange("p a v -> p (a v)")).then_inc(S("ret_rec"), 1)
                for k in range(3):
                    for d in range(2):
                        dst = k + 1 if d == 0 else 2 - k
                        dve.wait_ge(S("ret_rec"), 8 * p + 2 * k + d + 1)
                        ins = dve.scalar_tensor_tensor(Sr[:, dst, d, :], Sr[:, dst - 1 if d == 0 else dst + 1, d, :],
                                                       rtot[:, d, ds(p, 1)], kv[:, 2 + 3 * d + k, :], MUL, ADD)
                        ins.then_inc(S("ret_rec"), 1)
                for e in range(2):
                    yh = yret[:, 1:5, ds(p * 256 + e * 128, 128)]
                    dve.wait_ge(S("ret_yc"), 2 * p + e + 1)
                    dve.wait_ge(S("ret_i"), 2 * p + e + 1)
                    it = flat[:, 3072:4096].rearrange("p (c d v) -> p d c v", c=4, d=2)
                    for d in range(2):
                        if d:
                            dve.wait_ge(S("ret_rd"), 4 * p + 2 * e + 1)
                        dve.scalar_tensor_tensor(yh, it[:, d, :, :], rdec[:, d, ds(2 * p + e + 8 * d, 1)], yh,
                                                 MUL, ADD).then_inc(S("ret_rd"), 1)
                    dve.wait_ge(S("ret_rd"), 4 * p + 2 * e + 2)
                    for c in range(NCH):
                        ins = dve.bn_stats(bst[:, ds(2 * p + e, 1), c, :].rearrange("p a b -> p (a b)"),
                                           yret[:, c, ds(p * 256 + e * 128, 128)])
                    ins.then_inc(S("ret_bn"), 1)
            dve.wait_ge(S("ret_bn"), RH)
            for h in range(RH):
                for c in range(NCH):
                    ins = dve.bn_aggr(mv[:, h, c, :], bst[:, h, c, :])
            ins.then_inc(S("ret_ag"), 1)

        def act_ret_out(act):
            act.wait_ge(S("ret_ag"), 1)
            act.activation(rsd[:, :, :], mv[:, :, :, 1], ACT.Sqrt, bias=eps).then_inc(S("ret_sq"), 1)
            n0 = KT * APPLIED.index("retT")
            act.wait_ge(S("ret_nrm"), 40)
            for k in range(KT):
                act.wait_ge(S("tp_read"), tp_base["retT"] + k + 1)
                act.activation(h_hi[:, k, :], gT[:, k, :], ACT.Copy).then_inc(S("h_hi"), 1)

        def dve_ret_out(dve):
            dve.wait_ge(S("ret_sq"), 1)
            dve.reciprocal(rsd[:, :, :], rsd[:, :, :]).then_inc(S("ret_rc"), 1)
            dve.wait_ge(S("ret_rc"), 1)
            with dve.Fori(0, RH) as h:
                for c in range(NCH):
                    yc = yret[:, c, ds(h * 128, 128)]
                    dve.tensor_scalar(yc, yc, mv[:, ds(h, 1), c, 0], rsd[:, ds(h, 1), c], SUB, MUL).then_inc(S("ret_nrm"), 1)
            n0 = KT * APPLIED.index("retT")
            for k in range(KT + 1):
                if k < KT:
                    tp_full(dve, tpf_base["retT"] + k)
                    for (c0, c1), src in ((PROMPT, TP[:, 0, :]), (SAMPLE, TP[:, 1:5, :])):
                        g_ = gT[:, k, c0:c1]
                        if c0:
                            g_ = g_.rearrange("p (c t) -> p c t", c=4)
                        ins = dve.scalar_tensor_tensor(g_, src, gngain[:, k:k + 1], g_, MUL, MUL)
                    ins.then_inc(S("tp_read"), 1)
                if k:
                    dve.wait_ge(S("h_hi"), n0 + k)
                    dve.tensor_tensor(h_lo[:, k - 1, :], gT[:, k - 1, :], h_hi[:, k - 1, :].bitcast(F32), SUB).then_inc(S("h_ready"), 1)

        def pe_ret_out(pe):
            pe.wait_ge(S("ret_nrm"), 40)
            for k in range(KT):
                tp_free(pe, tp_base["retT"] + k)
                for c in range(NCH):
                    last = pe.transpose(TP[:, c, :], yret[:, c, ds(k * 128, 128)], ident)
                last.then_inc(S("tp_full"), 1)

        def pe_qkv(pe):
            s = stages["qkv"]
            ready = lambda r, k: (S(f"pj_read{(s.f0 + r) % 2}"), (s.f0 + r) // 2 + 1 + k)
            for r in range(2):
                pe_unit(pe, s, r, 0, 2, H, hready("norm10") if r == 0 else None)
            with pe.Fori(1, s.M // 2) as j:
                for r in range(2):
                    pe_unit(pe, s, r, j, 2, H)
                    pe_T(pe, "qkv", r - 2 + 2 * j, sT3[:, r, :], ready(r, j - 1))
            for r in range(2):
                pe_T(pe, "qkv", s.M - 2 + r, sT3[:, r, :], ready(s.M - 2 + r, 0))

        def act_qkv(act):
            s = stages["qkv"]

            def body(r, j):
                evac_wait(act, s, r, j)
                act_split(act, s.u0 + r + 2, j)
                if not (isinstance(j, int) and r < 2):
                    act.wait_ge(S("tp_full"), tpf_base["qkv"] + r - 1 + 4 * j)
                act.activation(two(sT3[:, r % 2, :]), pj(s.f0 + r), ACT.Copy).then_inc(tp_read(s, r), 1)

            for_units(act, s, body, peel=1)

        def dve_qkv(dve):
            s = stages["qkv"]

            def put(i):
                tp_full(dve, tpf_base["qkv"] + i)
                dst = qkv[:, :, i * 128:(i + 1) * 128] if isinstance(i, int) else qkv[:, :, ds(i * 128, 128)]
                dve.tensor_copy(dst, TP).then_inc(S("tp_read"), 1)

            def body(r, j):
                dve_split(dve, s.u0 + r + 2, j)
                if not (isinstance(j, int) and r < 2):
                    put(r - 2 + 4 * j)

            for_units(dve, s, body, peel=1)
            for i in range(s.M - 2, s.M):
                put(i)

        QK = (AH + AG) * AD

        def act_qk(act):
            act.wait_ge(S("tp_read"), tp_base["qkv"] + 12)
            for c in range(NCH):
                if c:
                    act.wait_ge(S("at_red"), c)
                act.activation(rt1[:, :], qkv[:, c, 0:QK], ACT.Square).then_inc(S("at_sq"), 1)
            act.wait_ge(S("at_red"), NCH)
            act.activation(astat[:, 1, :, :], astat[:, 0, :, :], ACT.Sqrt, bias=eps, scale=1.0 / AD).then_inc(S("at_sq"), 1)

        def dve_qk(dve):
            n = [0]

            def step(ins):
                n[0] += 1
                ins.then_inc(S("at_v"), 1)
                dve.wait_ge(S("at_v"), n[0])

            for c in range(NCH):
                dve.wait_ge(S("at_sq"), c + 1)
                dve.tensor_reduce(astat[:, 0, c, :], rt1[:, :].rearrange("p (h d) -> p h d", d=AD), AX.X, ADD).then_inc(S("at_red"), 1)
            dve.wait_ge(S("at_sq"), NCH + 1)
            step(dve.reciprocal(astat[:, 2, :, :], astat[:, 1, :, :]))
            for c in range(NCH):
                xc = qkv[:, c, 0:QK].rearrange("p (h d) -> p h d", d=AD)
                step(dve.tensor_tensor(xc, xc, astat[:, 2, c, :].unsqueeze(2).to_broadcast([128, AH + AG, AD]), MUL))
                for g, (h0, h1) in enumerate(((0, AH), (AH, AH + AG))):
                    ins = dve.tensor_tensor(xc[:, h0:h1, :], xc[:, h0:h1, :],
                                            qkgain[:, g:g + 1, :].to_broadcast([128, h1 - h0, AD]), MUL)
                step(ins)
                if c == 0:
                    continue
                dve.wait_ge(S("ld_rope"), 16)
                cos, sin = rope[:, 0, c - 1, :], rope[:, 1, c - 1, :]
                dve.tensor_tensor(rt1[:, :].rearrange("p (h d) -> p h d", d=AD), xc,
                                  cos.unsqueeze(1).to_broadcast([128, AH + AG, AD]), MUL)
                x5 = qkv[:, c, 0:QK].rearrange("p (h a b f) -> p h a b f", a=2, b=2, f=16)
                r5 = rt2[:, :].rearrange("p (h a b f) -> p h a b f", a=2, b=2, f=16)
                s4 = sin.rearrange("p (a b f) -> p a b f", a=2, b=2)
                for b in range(2):
                    ins = dve.tensor_tensor(r5[:, :, :, b, :], x5[:, :, :, 1 - b, :],
                                            s4[:, :, b, :].unsqueeze(1).to_broadcast([128, AH + AG, 2, 16]), MUL)
                step(ins)
                step(dve.tensor_tensor(qkv[:, c, 0:QK], rt1[:, :], rt2[:, :], ADD))
            assert n[0] == 1 + 2 * NCH + 2 * (NCH - 1)
            for m in range(12):
                tp_full(dve, tpf_base["qkT"] + m)
                if m < 8:
                    dve.tensor_scalar(qT[:, m, 0:128], TP[:, 0, :], AD ** -0.5, None, MUL)
                    dve.tensor_scalar(qT[:, m, 130:642].rearrange("p (c t) -> p c t", c=4), TP[:, 1:5, :], AD ** -0.5,
                                      None, MUL).then_inc(S("tp_read"), 1)
                else:
                    dve.tensor_copy(kT[:, m - 8, 0, :], TP[:, 0, :])
                    dve.tensor_copy(kT[:, m - 8, 2:6, :], TP[:, 1:5, :]).then_inc(S("tp_read"), 1)

        ROPED = 1 + 2 * NCH + 2 * (NCH - 1)

        def pe_qkT(pe):
            pe.wait_ge(S("at_v"), ROPED)
            for m in range(12):
                tp_free(pe, tp_base["qkT"] + m)
                for c in range(NCH):
                    if m < 8:
                        last = pe.transpose(TP[:, c, :], qkv[:, c, m * 128:(m + 1) * 128], ident)
                        continue
                    at = AH * AD + (m - 8) * AD
                    for half in range(2):
                        last = pe.matmul(TP[64 * half:64 * half + 64, c, :], qkv[:, c, at:at + AD], ident,
                                         start=True, stop=True)
                last.then_inc(S("tp_full"), 1)

        NG = NCH * AR
        CHUNKS = (1, 2, 3, 4, 0)
        PART_OF = ((0, 2), (2, 3), (3, 4), (4, 5))

        def place(n):
            return n // AR, CHUNKS[n // AR], n % AR

        def blocks(c):
            return (0, 1) if c == 0 else (1, 6)

        def width(c):
            return 128 * (blocks(c)[1] - blocks(c)[0])

        def pe_att(pe):
            t0 = tp_base["att"]
            pe.wait_ge(S("tp_read"), t0)
            pe.wait_ge(S("ld_past"), 32)
            all_read(pe, stages["qkv"].f0 + 12)

            for g in range(AG):
                def scores(n):
                    k, c, r = place(n)
                    rows, (b0, b1) = slice(64 * (r % 2), 64 * (r % 2) + 64), blocks(c)
                    pe.wait_ge(S("at_e"), NG * g + (n - 1 if n >= 2 else 0))
                    q = tile(qT, 2 * g + r // 2)[rows, chunk(c)]
                    o0 = 1024 * (n % 2)
                    for c0, c1 in ((b0, min(b1, b0 + 4)), (b0 + 4, b1)):
                        if c0 < c1:
                            last = pe.matmul(flat[:, o0 + (c0 - b0) * 128:o0 + (c1 - b0) * 128], q,
                                             kT[rows, g, c0:c1, :], start=True, stop=True)
                    last.then_inc(S("at_s"), 1)

                def trans(n):
                    k, c, r = place(n)
                    pe.wait_ge(S("at_p"), NG * g + n + 1)
                    tp_free(pe, t0 + NG * g + n)
                    for b in range(blocks(c)[1] - blocks(c)[0]):
                        last = pe.transpose(TP[:, b, :], Pr[:, n % 2, b * 128:(b + 1) * 128], ident)
                    last.then_inc(S("tp_full"), 1)

                def values(k, part):
                    c = CHUNKS[k]
                    b0, b1 = blocks(c)
                    p0, p1 = PART_OF[part]
                    if p0 == 0:
                        pe.wait_ge(S("tp_read"), t0 + NG * g + AR * k + AR)
                        pe.wait_ge(S("at_lo"), NCH * g + (k - 1 if k >= 2 else 0))
                    for b in range(b0 + p0, min(b0 + p1, b1)):
                        at = (AH + AG) * AD + g * AD
                        v = vpast[:, g * AD:(g + 1) * AD] if b == 1 else qkv[:, max(b - 1, 0), at:at + AD]
                        for par in range(2):
                            last = pe.matmul((B6, B7)[k % 2][64 * par:64 * par + 64, 0:256].rearrange("p (m t) -> p m t", m=2), v,
                                             PT[:, k % 2, b - b0, par:AR:2, :], start=(b == b0), stop=(b == b1 - 1))
                        if b == b1 - 1:
                            last.then_inc(S("at_o"), 1)

                scores(0)
                for n in range(NG):
                    if n + 1 < NG:
                        scores(n + 1)
                    if n >= AR:
                        values(n // AR - 1, n % AR)
                    trans(n)
                values(NCH - 1, 0)

        def act_att(act):
            t0, f0 = tp_base["att"], tpf_base["att"]
            with act.Fori(0, AG) as g:
                def probs(n):
                    k, c, r = place(n)
                    act.wait_ge(S("tp_full"), f0 + NG * g + (n - 1 if n >= 2 else 0))
                    act.wait_ge(S("at_m"), NG * g + n + 1)
                    act.activation(Pr[:, n % 2, 0:width(c)], flat[:, 1024 * (n % 2):1024 * (n % 2) + width(c)], ACT.Exp,
                                   bias=amax[:, n % 2, 0:1], accum_out=asum[:, n % 2, 0:1]).then_inc(S("at_e"), 1)

                def put(n):
                    k, c, r = place(n)
                    nb = blocks(c)[1] - blocks(c)[0]
                    tp_full(act, f0 + NG * g + n)
                    if k >= 2:
                        act.wait_ge(S("at_o"), NCH * g + k - 1)
                    act.activation(PT[:, k % 2, 0:nb, r, :], TP[:, 0:nb, :], ACT.Copy).then_inc(S("tp_read"), 1)

                def out(k):
                    act.wait_ge(S("at_o"), NCH * g + k + 1)
                    act.activation(h_hi[:, ds(2 * g, 2), chunk(CHUNKS[k])], (B6, B7)[k % 2][:, 0:256].rearrange("p (m t) -> p m t", m=2),
                                   ACT.Copy).then_inc(S("at_hi"), 1)

                probs(0)
                for n in range(NG):
                    if n + 1 < NG:
                        probs(n + 1)
                    put(n)
                    if n >= 2 * AR and n % AR == 0:
                        out(n // AR - 2)
                for k in range(NCH - 2, NCH):
                    out(k)

        def dve_att(dve):
            dve.wait_ge(S("at_v"), ROPED)
            for h in H:
                for at in EMPTY:
                    ins = dve.memset(h[:, :, at:at + 2].bitcast(F32), 0.0)
            ins.then_inc(S("at_empty"), 1)
            with dve.Fori(0, AG) as g:
                def top(n):
                    k, c, r = place(n)
                    dve.wait_ge(S("at_s"), NG * g + n + 1)
                    dve.tensor_reduce(amax[:, n % 2, 0:1], flat[:, 1024 * (n % 2):1024 * (n % 2) + width(c)], AX.X, MAX,
                                      negate=True).then_inc(S("at_m"), 1)

                def norm(n):
                    k, c, r = place(n)
                    w = width(c)
                    dve.wait_ge(S("at_e"), NG * g + n + 1)
                    dve.reciprocal(asum[:, n % 2, 1:2], asum[:, n % 2, 0:1]).then_inc(S("at_r"), 1)
                    dve.wait_ge(S("at_r"), NG * g + n + 1)
                    dve.tensor_scalar(Pr[:, n % 2, 0:w], Pr[:, n % 2, 0:w], asum[:, n % 2, 1:2], None, MUL).then_inc(S("at_p"), 1)

                def out(k):
                    dve.wait_ge(S("at_hi"), NCH * g + k + 1)
                    dve.tensor_tensor(h_lo[:, ds(2 * g, 2), chunk(CHUNKS[k])], (B6, B7)[k % 2][:, 0:256].rearrange("p (m t) -> p m t", m=2),
                                      h_hi[:, ds(2 * g, 2), chunk(CHUNKS[k])].bitcast(F32), SUB).then_inc(S("at_lo"), 1)

                top(0)
                for n in range(NG):
                    norm(n)
                    if n + 1 < NG:
                        top(n + 1)
                    if n >= 2 * AR and n % AR == 0:
                        out(n // AR - 2)
                for k in range(NCH - 2, NCH):
                    out(k)

        def gate(l, part):
            return lambda k, g: modcol(l, part, k, g)

        def gain(l, w):
            return lambda k, g: gains[:, l, w, k, g:g + 1]

        N_SMALL = 12
        block = ctx.enter_context(nc.Block())

        @block.sync
        def _(sp):
            sp.dma_start(cond[:, :, :], a["cond"]).then_inc(S("ld_cond"), 16)
            sp.dma_start(cst[:, :], a["consts"]).then_inc(S("ld_cst"), 16)
            for t, src in ((bmod, a["b_mod"]), (norms, a["norms"]), (ssmgain, a["ssm_gain"]), (gngain, a["gn_gain"]),
                           (fconv, a["ffn_conv"]), (sconv, a["ssm_conv"]), (dtp[:, 0:2], a["dt_params"]),
                           (lpair, a["decay_pair"])):
                sp.dma_start(t if t.__class__.__name__ == "AP" else t[tuple([slice(None)] * len(t.shape))], src).then_inc(S("ld_small"), 16)
            sp.dma_start(lrow[:, :], a["decay"].partition_broadcast(128)).then_inc(S("ld_small"), 16)
            sp.dma_start(drow[:, :, :], a["ssm_d"].partition_broadcast(128)).then_inc(S("ld_small"), 16)
            sp.dma_start(qkgain[:, :, :], a["qk_gain"].partition_broadcast(128)).then_inc(S("ld_small"), 16)
            sp.dma_start(x[:, :, :], a["x"]).then_inc(S("ld_small"), 16)
            for s in order:
                if s.name == "qkv":
                    sp.wait_ge(S("h_ready"), KT * (APPLIED.index("retT") + 1))
                    sp.dma_start(kT[:, :, 1, :], a["k_past"]).then_inc(S("ld_past"), 16)
                    sp.dma_start(vpast[:, :], a["v_past"]).then_inc(S("ld_past"), 16)
                if s.M // 4 >= 2:
                    for r in range(4):
                        sp_unit(sp, s, r, 0)
                    with sp.Fori(1, s.M // 4) as j:
                        for r in range(4):
                            sp_unit(sp, s, r, j)
                    rest = s.M // 4 * 4
                else:
                    rest = 0
                for r in range(rest, s.M):
                    sp_unit(sp, s, r, 0)
            all_read(sp, order[-1].f0 + 8)
            sp.dma_start(o["y"], x[:, :, :]).then_inc(S("st_y"), 16)
            sp.wait_ge(S("st_y"), 16)

        @block.scalar
        def _(act):
            act.wait_ge(S("ld_cond"), 16)
            act.activation(csil[:, :, :], cond[:, :, :], ACT.Silu).then_inc(S("csil"), 1)
            act.wait_ge(S("ld_cst"), 16)
            for r in range(2):
                act_split(act, stages["dt"].u0 + r)
            act.wait_ge(S("ld_small"), 16 * N_SMALL)
            act.activation(dtp[:, 1:2], dtp[:, 1:2], ACT.Exp).then_inc(S("dtp"), 1)
            for k in range(KT):
                act_square(act, "norm00", k, x[:, k, :])
            act_root(act, "norm00")
            act_apply(act, "norm00", gate(0, 0))
            act_dt(act)
            act_ssd_in(act)
            act.wait_ge(S("pe_unit"), stages["z"].u0 + 8)
            act.dma_start(s0[:, :, :, :], a["s_ssm"]).then_inc(S("ld_s0"), 16)
            act_cum(act)
            act_ssd(act)
            act.wait_ge(S("ssd_so"), SH)
            act.dma_start(o["s_ssm"], sout[:, :, :, :]).then_inc(S("st_ssm"), 16)
            act.wait_ge(S("st_ssm"), 16)
            act_apply(act, "again", gate(0, 0))
            act_ret_in(act)
            for k in range(KT):
                act_square(act, "normS", k, zT[:, k, :])
            act_root(act, "normS")
            act_apply(act, "normS")
            act_out_stage(act, stages["wo_ssm"])
            act_ret_setup(act)
            act.dma_start(s0r[:, :, :, :], a["s_ret"]).then_inc(S("ld_s0r"), 16)
            act_ret(act)
            act.wait_ge(S("ret_so"), 4)
            act.dma_start(o["s_ret"], soutr[:, :, :, :]).then_inc(S("st_ret"), 16)
            act.wait_ge(S("st_ret"), 16)
            act_ret_out(act)
            act_out_stage(act, stages["wo_ret"], "norm01")
            act_root(act, "norm01")
            act_apply(act, "norm01", gate(0, 3))
            for n in range(3):
                act_up(act, stages[f"up0{n}"], 0)
                act_out_stage(act, stages[f"dn0{n}"], "norm10" if n == 2 else None)
            act_root(act, "norm10")
            act_apply(act, "norm10", gate(1, 0))
            act_qkv(act)
            act.wait_ge(S("pe_unit"), stages["qkv"].u0 + 12)
            act.dma_start(rope[:, :, :, :], a["rope"]).then_inc(S("ld_rope"), 16)
            act_qk(act)
            act.wait_ge(S("at_v"), 3)
            act.dma_start(o["k"], qkv[:, 0, AH * AD:QK]).then_inc(S("st_kv"), 16)
            act.dma_start(o["v"], qkv[:, 0, QK:QK + AG * AD]).then_inc(S("st_kv"), 16)
            act_att(act)
            act_out_stage(act, stages["wo"], "norm11")
            act_root(act, "norm11")
            act_apply(act, "norm11", gate(1, 3))
            act.wait_ge(S("st_kv"), 32)
            for n in range(3):
                act_up(act, stages[f"up1{n}"], 1)
                act_out_stage(act, stages[f"dn1{n}"])

        @block.vector
        def _(dve):
            dve_setup(dve)
            dve_small(dve)
            for r in range(2):
                dve_split(dve, stages["dt"].u0 + r)
            dve_mod(dve, "modA", B6[:, 0:4 * KT])
            for k in range(KT):
                dve_add_square(dve, "norm00", k)
            dve_rstd(dve, "norm00")
            dve_apply(dve, "norm00", x, gain(0, 0), gate(0, 0))
            dve_dt(dve)
            dve_ssd_in(dve)
            dve_cum(dve)
            dve_ssd(dve)
            dve.wait_ge(S("st_ssm"), 16)
            dve_mod(dve, "modB", B7[:, MODB:MODB + 160])
            dve_apply(dve, "again", x, gain(0, 0), gate(0, 0))
            dve_ret_in(dve)
            for k in range(KT):
                dve_add_square(dve, "normS", k)
            dve_rstd(dve, "normS")
            dve.wait_ge(S("pe_unit"), stages["g"].u0 + 8)
            dve_apply(dve, "normS", zT, lambda k, g: ssmgain[:, k:k + 1], None)
            dve_out_stage(dve, stages["wo_ssm"], gate(0, 2))
            dve_ret_setup(dve)
            dve_ret(dve)
            dve_ret_out(dve)
            dve_out_stage(dve, stages["wo_ret"], gate(0, 2), "norm01")
            dve_rstd(dve, "norm01")
            dve_apply(dve, "norm01", x, gain(0, 1), gate(0, 3))
            for n in range(3):
                dve_up(dve, stages[f"up0{n}"], 0)
                dve_out_stage(dve, stages[f"dn0{n}"], gate(0, 5), "norm10" if n == 2 else None)
            dve_rstd(dve, "norm10")
            dve_apply(dve, "norm10", x, gain(1, 0), gate(1, 0))
            dve_qkv(dve)
            dve_qk(dve)
            dve_att(dve)
            dve_out_stage(dve, stages["wo"], gate(1, 2), "norm11")
            dve_rstd(dve, "norm11")
            dve_apply(dve, "norm11", x, gain(1, 1), gate(1, 3))
            for n in range(3):
                dve_up(dve, stages[f"up1{n}"], 1)
                dve_out_stage(dve, stages[f"dn1{n}"], gate(1, 5))

        @block.tensor
        def _(pe):
            pe.wait_ge(S("csil"), 1)
            pe_modA(pe)
            pe_norm(pe, "norm00")
            pe_unit(pe, stages["dt"], 0, 0, 2, H, hready("norm00"))
            pe_ssd_in(pe)
            pe_cum(pe)
            pe_ssd(pe)
            pe_spread(pe, "again")
            pe_ret_in(pe)
            pe_norm(pe, "normS")
            pe_stage(pe, stages["wo_ssm"], H, hready("normS"))
            pe_ret(pe)
            pe_ret_out(pe)
            pe_stage(pe, stages["wo_ret"], H, hready("retT"))
            pe_norm(pe, "norm01")
            for n in range(3):
                s = stages[f"up0{n}"]
                pe_stage(pe, s, H, hready("norm01") if n == 0 else None)
                pe_stage(pe, stages[f"dn0{n}"], HID, ("hid_ready", s.p0))
            pe_norm(pe, "norm10")
            pe_qkv(pe)
            pe_qkT(pe)
            pe_att(pe)
            pe.wait_ge(S("at_empty"), 1)
            pe.wait_ge(S("at_lo"), NCH * AG)
            pe_stage(pe, stages["wo"], H)
            pe_norm(pe, "norm11")
            for n in range(3):
                s = stages[f"up1{n}"]
                pe_stage(pe, s, H, hready("norm11") if n == 0 else None)
                pe_stage(pe, stages[f"dn1{n}"], HID, ("hid_ready", s.p0))
    return nc


def _tiles(w, cols=128):
    import numpy as np
    k, m = w.shape
    return np.ascontiguousarray(w.reshape(k // 128, 128, m // cols, cols).transpose(2, 1, 0, 3)).reshape(m // cols, 128, -1)


def _mod_units(w):
    import numpy as np
    n = w.shape[1] // 512
    return np.ascontiguousarray(w.reshape(4, 2, 128, n, 512).transpose(3, 0, 2, 1, 4)).reshape(4 * n, 128, 1024)


def _feat(v):
    import numpy as np
    v = v.reshape(v.shape[:-1] + (v.shape[-1] // 128, 128))
    return np.ascontiguousarray(np.moveaxis(v, -1, 0))


def kernel(x_prompt, x_sample, state_ret, state_ssm, cache_attn_k, cache_attn_v, c, c_ctx,
           w_mod, b_mod, norm_mix, norm_ffn, ffn_w_up, ffn_conv_w, ffn_conv_b, ffn_w_down,
           hyb_w_in, hyb_w_out, ret_log_decay, ret_gn_gain, ssm_conv_w, ssm_conv_b, ssm_a_log,
           ssm_dt_bias, ssm_d, ssm_norm_gain, attn_w_qkv, attn_q_gain, attn_k_gain, attn_w_o):
    import numpy as np
    import concourse.bacc as bacc
    from concourse.bass_utils import run_bass_kernel_spmd as run

    f32 = np.float32
    A = {}
    xf = np.zeros((128, KT, TOK), f32)
    xf[:, :, PROMPT[0]:PROMPT[1]] = _feat(x_prompt[0]).transpose(0, 2, 1)
    xf[:, :, SAMPLE[0]:SAMPLE[1]] = _feat(x_sample[0]).transpose(0, 2, 1)
    A["x"] = xf
    A["cond"] = np.ascontiguousarray(_feat(np.stack([c_ctx, c[0]])).transpose(0, 2, 1))
    A["consts"] = constants()
    A["rope"] = rope_tables()
    A["w_modA"] = _tiles(w_mod[0][:, :2 * D_MODEL])
    A["w_modB"] = _mod_units(np.concatenate([w_mod[0][:, 2 * D_MODEL:], w_mod[1]], 1))
    A["b_mod"] = _feat(b_mod)
    A["norms"] = _feat(np.stack([norm_mix, norm_ffn], 1))
    w = hyb_w_in[0]
    dt = np.zeros((D_MODEL, 128), f32)
    for at in range(0, 128, 32):
        dt[:, at:at + SH] = w[:, 6144:6160]
    A["hyb_in"] = _tiles(np.concatenate([dt, w[:, 4096:6144], w[:, 3072:4096], w[:, 0:3072]], 1))
    A["hyb_out"] = np.stack([_tiles(hyb_w_out[0][h * 1024:(h + 1) * 1024]) for h in range(2)])
    up = ffn_w_up.reshape(2, D_MODEL, 2, FT, 128).transpose(0, 1, 3, 2, 4).reshape(2, D_MODEL, 2 * FFN)
    A["ffn_up"] = np.stack([_tiles(w_) for w_ in up])
    A["ffn_down"] = np.stack([_tiles(w_) for w_ in ffn_w_down])
    fc = np.concatenate([ffn_conv_w, ffn_conv_b[:, None]], 1).reshape(2, 4, 2, FT, 128)
    A["ffn_conv"] = np.ascontiguousarray(fc.transpose(4, 0, 3, 2, 1)).reshape(128, 2, 2 * FT, 4)
    sc = np.concatenate([ssm_conv_w[0], ssm_conv_b], 0).reshape(4, 16, 128)
    A["ssm_conv"] = np.ascontiguousarray(sc.transpose(2, 1, 0))
    A["ssm_gain"] = _feat(ssm_norm_gain[0])
    A["gn_gain"] = _feat(ret_gn_gain[0])
    dp = np.zeros((128, 2), f32)
    for at in range(0, 128, 64):
        for d in range(2):
            dp[at + 32 * d:at + 32 * d + SH, 0] = ssm_dt_bias[0, d]
            if at:
                dp[at + 32 * d:at + 32 * d + SH, 1] = ssm_a_log[0, d]
    A["dt_params"] = dp
    A["decay"] = np.ascontiguousarray(ret_log_decay[0].reshape(16))
    A["decay_pair"] = np.ascontiguousarray(np.repeat(ret_log_decay[0].reshape(2, 4, 2).transpose(2, 0, 1), 64, 0))
    A["ssm_d"] = np.ascontiguousarray(ssm_d[0])
    A["qk_gain"] = np.stack([attn_q_gain[0], attn_k_gain[0]])
    A["qkv"] = _tiles(attn_w_qkv[0])
    A["attn_o"] = _tiles(attn_w_o[0])
    kp = cache_attn_k[0, 0].transpose(2, 1, 0)
    A["k_past"] = np.ascontiguousarray(np.concatenate([kp, kp], 0))
    A["v_past"] = np.ascontiguousarray(cache_attn_v[0, 0].reshape(PAST, AG * AD))
    sr = state_ret[0, 0].reshape(2, 4, 2, 64, 128)
    A["s_ret"] = np.ascontiguousarray(sr.transpose(2, 3, 1, 0, 4)).reshape(128, 4, 2, 128)
    A["s_ssm"] = np.ascontiguousarray(state_ssm[0, 0].transpose(2, 0, 1, 3))

    nc = bacc.Bacc("TRN2", target_bir_lowering=False, num_devices=1, dynamic_dma_scratch_size=1024)
    f = mybir.dt.float32
    ins, arrays = {}, {}
    for name, v in A.items():
        v = np.ascontiguousarray(v, dtype=f32)
        arrays[f"in_{name}"] = v
        ins[name] = nc.dram_tensor(f"in_{name}", v.shape, f, kind="ExternalInput").ap()
    shapes = {"y": (128, KT, TOK), "s_ssm": (128, 2, SH, 64), "s_ret": (128, 2, 4, 128), "k": (128, 256), "v": (128, 256)}
    outs = {n: nc.dram_tensor(f"out_{n}", s, f, kind="ExternalOutput").ap() for n, s in shapes.items()}
    build(nc, ins, outs)
    r = run(nc, [arrays], core_ids=[0]).results[0]
    y = r["out_y"].transpose(2, 1, 0).reshape(TOK, D_MODEL)
    s_ret = r["out_s_ret"].reshape(2, 64, 2, 4, 128).transpose(2, 3, 0, 1, 4).reshape(1, 1, 2, RH, RDK, RDV)
    return (np.ascontiguousarray(y[PROMPT[0]:PROMPT[1]])[None], np.ascontiguousarray(y[SAMPLE[0]:SAMPLE[1]])[None],
            np.ascontiguousarray(s_ret),
            np.ascontiguousarray(r["out_s_ssm"].transpose(1, 2, 0, 3))[None, None],
            r["out_k"].reshape(1, 1, SEQ, AG, AD), r["out_v"].reshape(1, 1, SEQ, AG, AD))
```

```python
import concourse.bass as bass
from concourse import mybir
from contextlib import ExitStack

D_MODEL, SEQ, DEC, PAST = 1024, 128, 512, 128
KT = D_MODEL // 128
FFN = 2816
FT = FFN // 128
PARTS = [8, 7, 7]
FIRST = [0, 8, 15]
NCH = 5
TOK = 644
HALF = TOK // 2
COL = [0, 130, 258, 386, 514]
PROMPT, SAMPLE = (0, 128), (130, 642)
EMPTY = (128, 642)
RH, RDK, RDV = 8, 64, 128
SH, SG, SR, SN, SP_ = 16, 4, 4, 128, 64
AH, AG, AR, AD = 16, 4, 4, 64
EPS = 1e-6
UNIT = 1024
RAW = 4

C_ID, C_TRIF, C_TRIB, C_NEGF, C_NEGB, C_IJF, C_IJB, C_ONES, C_ID2 = [128 * n for n in range(9)]
C_COMB = C_ID2 + 64
C_SIGN = C_COMB + 2
C_RPOS = C_SIGN + 1
C_EPS = C_RPOS + 4
C_ALL = C_EPS + 1


def constants():
    import numpy as np
    c = np.zeros((128, C_ALL), np.float32)
    j, i = np.meshgrid(np.arange(128), np.arange(128), indexing="ij")
    c[:, C_ID:C_ID + 128] = j == i
    c[:, C_TRIF:C_TRIF + 128] = j <= i
    c[:, C_TRIB:C_TRIB + 128] = j >= i
    c[:, C_NEGF:C_NEGF + 128] = np.where(j <= i, 0, -1e30)
    c[:, C_NEGB:C_NEGB + 128] = np.where(j >= i, 0, -1e30)
    c[:, C_IJF:C_IJF + 128] = np.maximum(i - j, 0)
    c[:, C_IJB:C_IJB + 128] = np.maximum(j - i, 0)
    c[:, C_ONES:C_ONES + 128] = 1
    c[:, C_ID2:C_ID2 + 64] = (np.arange(128)[:, None] % 64) == np.arange(64)[None]
    c[0:4, C_COMB:C_COMB + 2] = np.array([[1, 0], [0, 1], [1, 0], [0, 1]])
    for r in (0, 32):
        c[r:r + SH, C_SIGN] = 1
        c[64 + r:64 + r + SH, C_SIGN] = -1
    n = np.arange(128)
    for k, v in enumerate((n + 1, 128 - n, 127 - n, n)):
        c[:, C_RPOS + k] = v
    c[:, C_EPS] = EPS
    return c


def rope_tables():
    import numpy as np
    inv = np.float32(10000.0) ** (-np.arange(16, dtype=np.float32) / np.float32(16))
    t = np.arange(DEC)
    ang = np.stack([(t // 64).astype(np.float32)[:, None] * inv, (t % 64).astype(np.float32)[:, None] * inv], 1)
    cos = np.repeat(np.cos(ang)[:, :, None], 2, 2)
    sin = np.stack([-np.sin(ang), np.sin(ang)], 2)
    both = np.stack([cos, sin], 0).reshape(2, 4, 128, 64)
    return np.ascontiguousarray(both.transpose(2, 0, 1, 3)).astype(np.float32)


def build(nc, a, o):
    F32, F32R = mybir.dt.float32, mybir.dt.float32r
    ACT, ALU, AX = mybir.ActivationFunctionType, mybir.AluOpType, mybir.AxisListType
    ds = bass.ds
    ADD, SUB, MUL, MAX, MIN = ALU.add, ALU.subtract, ALU.mult, ALU.max, ALU.min

    class Stage:
        pass

    stages, order = {}, []

    def stage(name, K, M, src, fm=True):
        s = Stage()
        s.name, s.K, s.M, s.src, s.fm = name, K, M, src, fm
        s.u0 = sum(t.M for t in order)
        s.f0 = sum(t.M for t in order if t.fm)
        stages[name] = s
        order.append(s)

    hyb = a["hyb_in"]
    stage("modA", KT, 2 * KT, a["w_modA"], fm=False)
    stage("dt", KT, 1, hyb[0:1])
    stage("xs", KT, 8, hyb[1:9])
    stage("bc", KT, 8, hyb[9:17])
    stage("z", KT, 8, hyb[17:25])
    stage("modB", KT, 96 - 2 * KT, a["w_modB"], fm=False)
    stage("qk", KT, 8, hyb[25:33])
    stage("v", KT, 8, hyb[33:41])
    stage("g", KT, 8, hyb[41:49])
    stage("wo_ssm", KT, 8, a["hyb_out"][1])
    stage("wo_ret", KT, 8, a["hyb_out"][0])

    def ffn_stages(l):
        for n, (first, K) in enumerate(zip(FIRST, PARTS)):
            stage(f"up{l}{n}", KT, 2 * K, a["ffn_up"][l, 2 * first:2 * (first + K)])
            stage(f"dn{l}{n}", K, 8, a["ffn_down"][l][:, :, first * 128:(first + K) * 128])

    ffn_stages(0)
    stage("qkv", KT, 12, a["qkv"])
    stage("wo", KT, 8, a["attn_o"])
    ffn_stages(1)
    KOF = [s.K for s in order for _ in range(s.M)]
    UNITS = len(KOF)

    tp_base, tpf_base, n, full = {}, {}, 0, 0
    for name, uses in (("norm00", 1), ("xs", 8), ("b", 4), ("da", 1), ("cumT", 1), ("ssd", 12), ("again", 1),
                       ("k", 4), ("v", 8), ("normS", 1), ("retT", 8), ("norm01", 1),
                       ("norm10", 1), ("qkv", 12), ("qkT", NCH), ("att", AG * NCH * AR), ("norm11", 1)):
        tp_base[name], tpf_base[name] = n, full
        n += uses
        full += uses

    ctx = ExitStack()
    with ctx:
        sems = {}

        def S(name):
            if name not in sems:
                sems[name] = ctx.enter_context(nc.semaphore(name))
            return sems[name]

        def sb(name, shape, dt=F32):
            return ctx.enter_context(nc.sbuf_tensor(name, shape, dt))

        cst = sb("cst", [128, C_ALL])
        ident = cst[:, C_ID:C_ID + 128]
        tri = [cst[:, C_TRIF:C_TRIF + 128], cst[:, C_TRIB:C_TRIB + 128]]
        ones = cst[:, C_ONES:C_ONES + 128]
        eps = cst[:, C_EPS:C_EPS + 1]
        x = sb("x", [128, KT, TOK])
        raw = sb("raw", [128, RAW, UNIT])
        w_hi, w_lo = sb("w_hi", [128, 2, UNIT], F32R), sb("w_lo", [128, 2, UNIT], F32R)
        cond, csil = sb("cond", [128, KT, 2]), sb("csil", [128, KT, 2])
        cond_r = sb("cond_r", [128, KT, 128], F32R)
        modrow = sb("modrow", [4, 2, 512])
        modT = sb("modT", [128, 2, 48, 2])
        bmod = sb("bmod", [128, 2, 48])
        norms = sb("norms", [128, 2, 2, KT])
        gains = sb("gains", [128, 2, 2, KT, 2])
        ssmgain, gngain = sb("ssmgain", [128, KT]), sb("gngain", [128, KT])
        fconv, sconv = sb("fconv", [128, 2, 2 * FT, 4]), sb("sconv", [128, 16, 4])
        ident_r = sb("ident_r", [128, 128], F32R)
        id2_r, nid2_r = sb("id2_r", [128, 64], F32R), sb("nid2_r", [128, 64], F32R)
        neg_r = sb("neg_r", [128, 2, 128], F32R)
        mv, rsd = sb("mv", [128, RH, NCH, 2]), sb("rsd", [128, RH, NCH])
        ssq, rs = sb("ssq", [128, TOK]), sb("rs", [128, 2, NCH])
        hf2 = sb("hf2", [128, 2, TOK])
        u_sb, t_sb = sb("u_sb", [128, 2, TOK]), sb("t_sb", [128, 2, TOK])
        sq, tn = u_sb, t_sb
        dtp = sb("dtp", [128, 3])
        lrow, lpair = sb("lrow", [128, 16]), sb("lpair", [128, 2, 4])
        drow, dsum = sb("drow", [128, 2, SH]), sb("dsum", [128, SH])
        qkgain = sb("qkgain", [128, 2, 64])

        H_BYTES = 2 * KT * TOK * 4
        h_hi, h_lo = sb("h_hi", [128, KT, TOK], F32R), sb("h_lo", [128, KT, TOK], F32R)
        H0 = nc.sbuf_base - H_BYTES
        A0 = nc.sbuf_base
        arena = sb("arena", [128, (nc.sbuf_bytes_remaining - 64) // 4])
        A_BYTES = (arena.shape[1]) * 4

        class Region:

            def __init__(self, at, size):
                self.at, self.end = at, at + size

            def __call__(self, name, shape, dt=F32):
                n = 4
                for k in shape[1:]:
                    n *= k
                n = -(-n // 32) * 32
                assert self.at + n <= self.end, (name, self.at + n - self.end)
                t = nc.alloc_sbuf_tensor_at(name, shape, dt, offset=self.at)
                self.at += n
                return t

        A = Region(A0, A_BYTES)
        zT = A("zT", [128, KT, TOK])
        mark = A.at
        bcT = A("bcT", [128, 8, TOK])
        xsTM = A("xsTM", [128, NCH, 1024])
        bTM = A("bTM", [128, NCH, 512])
        daT, da1, da2 = A("daT", [128, TOK]), A("da1", [128, TOK]), A("da2", [128, TOK])
        st_at = A.at
        sT = A("sT", [128, 2, TOK])
        daTM = A("daTM", [128, NCH, 128])
        B = Region(H0, H_BYTES)
        ecum, etot, wdt = B("ecum", [128, NCH, 64]), B("etot", [128, NCH, 64]), B("wdt", [128, NCH, 64])
        cum_r = B("cum_r", [128, NCH, 128], F32R)
        E = B("E", [128, 2, NCH, 128])
        GT = B("GT", [128, NCH, 128])
        xv = B("xv", [128, 2, 4, NCH, 64])
        Sst = B("Sst", [128, 2, 4, 2, 64])
        s0 = B("s0", [128, 2, SH, 64])
        inter = B("inter", [128, 2, 4, 64])
        sout = A("sout", [128, 2, SH, 64])
        yb = Region(st_at, 2 * TOK * 4)("yb", [128, 2, NCH, 128])
        A = Region(mark, A0 + A_BYTES - mark)
        qkT = A("qkT", [128, 8, TOK])
        kTM, vTM = A("kTM", [128, NCH, 512]), A("vTM", [128, NCH, 1024])
        gT = A("gT", [128, KT, TOK])
        sT2 = u_sb
        yret = Region(A0, mark - A0)("yret", [128, NCH, 1024])
        B = Region(H0, H_BYTES)
        mTf, mTb = B("mTf", [128, RH, 128]), B("mTb", [128, RH, 128])
        PTr = B("PTr", [128, 2, NCH, 128])
        kw = B("kw", [128, 2, NCH, 128])
        Sr = B("Sr", [128, 4, 2, 128])
        s0r, soutr = B("s0r", [128, 4, 2, 128]), B("soutr", [128, 2, 4, 128])
        rdec = B("rdec", [128, 4, 16])
        rtot = B("rtot", [128, 2, 4])
        bst = B("bst", [128, RH, NCH, 6])
        A = Region(A0, A_BYTES)
        qkv = A("qkv", [128, NCH, 1536])
        qT = A("qT", [128, KT, TOK])
        kT = A("kT", [128, AG, 6, 128])
        vpast = A("vpast", [128, 256])
        mark = A.at
        PT = A("PT", [128, 2, NCH, AR, 128])
        Pr = A("Pr", [128, 2, 640])
        amax, asum = A("amax", [128, 2, 4]), A("asum", [128, 2, 2])
        sT3 = Region(mark, 99999)("sT3", [128, 2, TOK])
        W = Region(mark, 99999)
        rt1, rt2 = W("rt1", [128, 1280]), W("rt2", [128, 1280])
        astat = W("astat", [128, 3, NCH, 20])
        rope = Region(H0, H_BYTES)("rope", [128, 2, 4, 64])
        A = Region(A0, A_BYTES)
        hid_hi, hid_lo = A("hid_hi", [128, 8, TOK], F32R), A("hid_lo", [128, 8, TOK], F32R)

        ps = ctx.enter_context(nc.psum_tensor("ps", [128, 8, 512], F32))

        def pj(f):
            return ps[:, 2 * (f % 2):2 * (f % 2) + 2, 0:HALF]

        flat = ps[:, :, :].rearrange("p b c -> p (b c)")
        TP = flat[:, 2048:2048 + 640].rearrange("p (c t) -> p c t", c=NCH)
        B6, B7 = flat[:, 3072:3584], flat[:, 3584:4096]

        def two(ap):
            return ap.rearrange("p (h c) -> p h c", h=2)

        def tile(t, k):
            return t[:, ds(k, 1), :].rearrange("p a c -> p (a c)")

        def chunk(c):
            return slice(COL[c], COL[c] + 128)

        def for_units(eng, s, body, step=4, peel=0, look=2):
            n = 0
            while step * (n + 1) <= s.M and all(
                s.u0 + step * n + r + look < UNITS and KOF[s.u0 + step * n + r + look] == s.K for r in range(step)
            ):
                n += 1
            if n < peel + 2:
                n = 0
            if n:
                for r in range(step * peel):
                    body(r, 0)
                with eng.Fori(peel, n) as j:
                    for r in range(step):
                        body(r, j)
            for r in range(step * n, s.M):
                body(r, 0)

        def sp_unit(sp, s, r, j):
            b = s.u0 + r
            if b >= RAW or not isinstance(j, int):
                sp.wait_ge(S("w_lo"), b - RAW + 1 + 4 * j)
            sp.dma_start(raw[:, b % RAW, 0:s.K * 128],
                         s.src[ds(r + 4 * j, 1)].rearrange("a p n -> (a p) n")).then_inc(S(f"w_in{b % RAW}"), 16)

        def act_split(act, b, j=0):
            if b >= UNITS:
                return
            n, i = KOF[b] * 128, b
            if i >= 2:
                act.wait_ge(S("pe_unit"), b - 1 + 4 * j)
            act.wait_ge(S(f"w_in{b % RAW}"), 16 * (b // RAW + 1) + 16 * j)
            act.activation(w_hi[:, i % 2, 0:n], raw[:, b % RAW, 0:n], ACT.Copy).then_inc(S("w_hi"), 1)

        def dve_split(dve, b, j=0):
            if b >= UNITS:
                return
            n, i = KOF[b] * 128, b
            dve.wait_ge(S("w_hi"), i + 1 + 4 * j)
            dve.tensor_tensor(w_lo[:, i % 2, 0:n], raw[:, b % RAW, 0:n], w_hi[:, i % 2, 0:n].bitcast(F32),
                              SUB).then_inc(S("w_lo"), 1)

        def pe_tile(pe, s, r, k, i, f, X):
            for n, (w, v) in enumerate(((w_hi, X[0]), (w_hi, X[1]), (w_lo, X[0]))):
                for hh in range(2):
                    last = pe.matmul(pj(f)[:, hh, :], w[:, i % 2, k * 128:(k + 1) * 128], v[:, k, hh * HALF:(hh + 1) * HALF],
                                     start=(k == 0 and n == 0), stop=(k == s.K - 1 and n == 2))
            return last

        def pe_unit(pe, s, r, j, X):
            b, f = s.u0 + r, s.f0 + r
            pe.wait_ge(S("w_lo"), b + 1 + 2 * j)
            if f >= 2 or not isinstance(j, int):
                pe.wait_ge(S(f"pj_read{f % 2}"), f // 2 + j)
            for k in range(s.K):
                last = pe_tile(pe, s, r, k, b, f, X)
            last.then_inc(S("pe_unit"), 1)

        def pe_first(pe, units, X, ready):
            for s, r in units:
                b, f = s.u0 + r, s.f0 + r
                pe.wait_ge(S("w_lo"), b + 1)
                if f >= 2:
                    pe.wait_ge(S(f"pj_read{f % 2}"), f // 2)
            for k in range(s.K):
                pe.wait_ge(S(ready[0]), ready[1] + k + 1)
                for s, r in units:
                    last = pe_tile(pe, s, r, k, s.u0 + r, s.f0 + r, X)
                    if k == s.K - 1:
                        last.then_inc(S("pe_unit"), 1)

        def evac_wait(eng, s, r, j, step=4):
            eng.wait_ge(S("pe_unit"), s.u0 + r + 1 + step * j)

        def tp_read(s, r):
            return S(f"pj_read{(s.f0 + r) % 2}")

        def all_read(eng, f):
            for q in range(2):
                if (f + 1 - q) // 2:
                    eng.wait_ge(S(f"pj_read{q}"), (f + 1 - q) // 2)

        def tp_free(pe, t):
            pe.wait_ge(S("tp_read"), t)

        def tp_full(eng, t):
            eng.wait_ge(S("tp_full"), t + 1)

        H, HID = (h_hi, h_lo), (hid_hi, hid_lo)
        ROWS = flat[:, 1536:2048]

        MA = stages["modA"].M
        COLS0 = 320

        def pe_mod_unit(pe, m):
            q, r = m // 4, m % 4
            b = stages["modA"].u0 + m if m < MA else stages["modB"].u0 + m - MA
            pe.wait_ge(S("w_lo"), b + 1)
            if r == 0 and q:
                pe.wait_ge(S("mod_rows"), q)
            for k in range(2):
                for n, w in enumerate((w_hi, w_lo)):
                    last = pe.matmul(ROWS, cond_r[:, 2 * r + k, :], w[:, b % 2, k * 512:(k + 1) * 512],
                                     start=(r + k + n == 0), stop=(r == 3 and k == 1 and n == 1))
            last.then_inc(S("pe_unit"), 1)

        def pe_mod_cols(pe, q):
            slot = (q if q < MA // 4 else (q - MA // 4) % 5) % 2
            pe.wait_ge(S("mod_rows"), q + 1)
            for c in range(4):
                at = COLS0 + 8 * q + 2 * c
                last = pe.matmul(B7[:, at:at + 2], modrow[0:4, slot, c * 128:(c + 1) * 128],
                                 cst[0:4, C_COMB:C_COMB + 2], start=True, stop=True)
            last.then_inc(S("mod_cols"), 1)

        def pe_modA(pe):
            for m in range(MA):
                pe_mod_unit(pe, m)
                if m % 4 == 1 and m > 4:
                    pe_mod_cols(pe, m // 4 - 1)
            pe_mod_cols(pe, MA // 4 - 1)

        def act_modA(act):
            for m in range(MA):
                act_split(act, m + 2)
                if m % 4 == 3:
                    act.wait_ge(S("pe_unit"), m + 1)
                    if m >= 8:
                        act.wait_ge(S("mod_cols"), m // 4 - 1)
                    act.activation(modrow[:, m // 4 % 2, :], ROWS[0:4, :], ACT.Copy).then_inc(S("mod_rows"), 1)

        def act_modB(act, m, g):
            b, q = stages["modB"].u0 + m, m // 4
            act_split(act, b + 2, 5 * g)
            if m % 4 == 3:
                act.wait_ge(S("pe_unit"), b + 1 + 20 * g)
                if m >= 8:
                    act.wait_ge(S("mod_cols"), MA // 4 + q - 1 + 5 * g)
                act.activation(modrow[:, q % 2, :], ROWS[0:4, :], ACT.Copy).then_inc(S("mod_rows"), 1)

        ALL_MODS = modT[:, :, :, :].rearrange("p l m g -> p (l m) g")
        ALL_BIAS = bmod[:, :, :].rearrange("p l m -> p (l m)")

        def dve_mod(dve, name):
            s = stages[name]
            t0, t1 = (0, s.M) if name == "modA" else (stages["modA"].M, 96)
            dve.wait_ge(S("mod_cols"), t1 // 4)
            src = B7[:, COLS0 + 2 * t0:COLS0 + 2 * t1].rearrange("p (m g) -> p m g", g=2)
            dve.tensor_tensor(ALL_MODS[:, t0:t1, :], src,
                              ALL_BIAS[:, t0:t1].unsqueeze(2).to_broadcast([128, t1 - t0, 2]), ADD).then_inc(S("mod"), 1)
            dve.wait_ge(S("mod"), 1 if name == "modA" else 3)
            for l, w in ((0, 0),) if name == "modA" else ((0, 1), (1, 0), (1, 1)):
                part = modT[:, l, (3 * w + 1) * KT:(3 * w + 2) * KT, :]
                ins = dve.scalar_tensor_tensor(gains[:, l, w, :, :], part, 1.0,
                                               norms[:, l, w, :].unsqueeze(2).to_broadcast([128, KT, 2]), ADD, MUL)
            ins.then_inc(S("mod"), 1)
            dve.wait_ge(S("mod"), 2 if name == "modA" else 4)

        def modcol(l, part, k, g):
            return modT[:, l, part * KT + k, g:g + 1]

        NORMS = ["norm00", "normS", "norm01", "norm10", "norm11"]
        APPLIED = ["norm00", "again", "normS", "retT", "norm01", "norm10", "norm11"]
        BY_RSTD = [p for p in APPLIED if p != "retT"]

        def act_square(act, name, k, src_k, ready=None):
            n = KT * NORMS.index(name) + k
            if ready:
                act.wait_ge(*ready)
            if n >= 2:
                act.wait_ge(S("sq_add"), n - 1)
            act.activation(sq[:, k % 2, :], src_k, ACT.Square).then_inc(S("sq"), 1)

        def dve_add_square(dve, name, k):
            n = KT * NORMS.index(name) + k
            dve.wait_ge(S("sq"), n + 1)
            if n:
                dve.wait_ge(S("sq_add"), n)
            if k == 0:
                dve.tensor_copy(ssq[:, :], sq[:, 0, :]).then_inc(S("sq_add"), 1)
            else:
                dve.tensor_tensor(ssq[:, :], ssq[:, :], sq[:, k % 2, :], ADD).then_inc(S("sq_add"), 1)

        MS = flat[:, 2048 + 640:2048 + 640 + NCH]

        def pe_norm(pe, name):
            pe.wait_ge(S("sq_add"), KT * (NORMS.index(name) + 1))
            tp_free(pe, tp_base[name])
            for c in range(NCH):
                last = pe.matmul(MS[:, c:c + 1], ssq[:, chunk(c)], ones[:, 0:1], start=True, stop=True)
            last.then_inc(S("ms"), 1)
            pe_spread(pe, name)

        def pe_spread(pe, name):
            pe.wait_ge(S("rstd"), 1 if name == "again" else NORMS.index(name) + 1)
            tp_free(pe, tp_base[name])
            for c in range(NCH):
                last = pe.matmul(TP[:, c, :], rs[:, 1, c:c + 1].to_broadcast([128, 128]), ident, start=True, stop=True)
            last.then_inc(S("tp_full"), 1)

        def act_root(act, name):
            act.wait_ge(S("ms"), NORMS.index(name) + 1)
            act.activation(rs[:, 0, :], MS, ACT.Sqrt, bias=eps, scale=1.0 / D_MODEL).then_inc(S("root"), 1)

        def dve_rstd(dve, name):
            dve.wait_ge(S("root"), NORMS.index(name) + 1)
            dve.reciprocal(rs[:, 1, :], rs[:, 0, :]).then_inc(S("rstd"), 1)

        GROUPS = ((PROMPT, 0), (SAMPLE, 128))

        def dve_apply(dve, name, src, scale, shift):
            n0, m0 = KT * APPLIED.index(name), KT * BY_RSTD.index(name)
            for h in H:
                for at in EMPTY:
                    dve.memset(h[:, :, at:at + 2].bitcast(F32), 0.0)
            tp_full(dve, tpf_base[name])
            for k in range(KT + 1):
                if k < KT:
                    if k == 0 and n0:
                        dve.wait_ge(S("h_hi"), n0)
                    if k >= 2:
                        dve.wait_ge(S("h_ready"), n0 + k - 1)
                    for g, ((c0, c1), at) in enumerate(GROUPS):
                        ins = dve.scalar_tensor_tensor(tn[:, k % 2, c0:c1], src[:, k, c0:c1], scale(k, g),
                                                       flat[:, 2048 + at:2048 + at + c1 - c0], MUL, MUL)
                    ins.then_inc(S("tn"), 1)
                if k:
                    dve.wait_ge(S("h_hi"), n0 + k)
                    for g, ((c0, c1), at) in enumerate(GROUPS):
                        hi = h_hi[:, k - 1, c0:c1].bitcast(F32)
                        if shift is None:
                            ins = dve.tensor_tensor(h_lo[:, k - 1, c0:c1], tn[:, (k - 1) % 2, c0:c1], hi, SUB)
                        else:
                            ins = dve.scalar_tensor_tensor(h_lo[:, k - 1, c0:c1], tn[:, (k - 1) % 2, c0:c1],
                                                           shift(k - 1, g), hi, ADD, SUB)
                    ins.then_inc(S("h_ready"), 1)
            dve.memset(ssq[:, 0:1], 0.0).then_inc(S("tp_read"), 1)

        def act_apply(act, name, shift=None):
            m0 = KT * BY_RSTD.index(name)
            for k in range(KT):
                act.wait_ge(S("tn"), m0 + k + 1)
                for g, ((c0, c1), at) in enumerate(GROUPS):
                    if shift is None:
                        ins = act.activation(h_hi[:, k, c0:c1], tn[:, k % 2, c0:c1], ACT.Copy)
                    else:
                        ins = act.activation(h_hi[:, k, c0:c1], tn[:, k % 2, c0:c1], ACT.Identity, bias=shift(k, g))
                ins.then_inc(S("h_hi"), 1)

        def hready(name):
            return ("h_ready", KT * APPLIED.index(name))

        def act_conv_in(act, s, r, j, cw):
            c = s.c0 + r
            if c >= 2:
                act.wait_ge(S("cv_done"), c - 1 + 4 * j)
            act.activation(two(u_sb[:, r % 2, :]), pj(s.f0 + r), ACT.Copy).then_inc(S("cv_u"), 1)
            act.activation(two(t_sb[:, r % 2, :]), pj(s.f0 + r), ACT.Identity, bias=cw[:, r + 4 * j, 3:4] if isinstance(j, int) else cw[:, ds(r + 4 * j, 1), 3],
                           scale=cw[:, r + 4 * j, 1:2] if isinstance(j, int) else cw[:, ds(r + 4 * j, 1), 1]).then_inc(tp_read(s, r), 1)

        def dve_conv(dve, s, r, j, cw):
            c, p, f = s.c0 + r, r % 2, s.f0 + r
            def w(n):
                return cw[:, r + 4 * j, n:n + 1] if isinstance(j, int) else cw[:, ds(r + 4 * j, 1), n]
            dve.wait_ge(tp_read(s, r), f // 2 + 1 + 2 * j)
            dve.scalar_tensor_tensor(t_sb[:, p, 1:TOK], u_sb[:, p, 0:TOK - 1], w(0), t_sb[:, p, 1:TOK],
                                     MUL, ADD).then_inc(S("cv_mid"), 1)
            dve.wait_ge(S("cv_mid"), c + 1 + 4 * j)
            dve.scalar_tensor_tensor(t_sb[:, p, 0:TOK - 1], u_sb[:, p, 1:TOK], w(2), t_sb[:, p, 0:TOK - 1],
                                     MUL, ADD).then_inc(S("cv_done"), 1)

        c = 0
        for name in ["xs", "bc"] + [f"up{l}{n}" for l in range(2) for n in range(3)]:
            stages[name].c0 = c
            c += stages[name].M
        c = 0
        for name in [f"up{l}{n}" for l in range(2) for n in range(3)]:
            stages[name].p0 = c
            c += stages[name].M // 2

        def pe_T(pe, name, i, src, ready):
            pe.wait_ge(*ready)
            tp_free(pe, tp_base[name] + i)
            for c in range(NCH):
                last = pe.transpose(TP[:, c, :], src[:, chunk(c)], ident)
            last.then_inc(S("tp_full"), 1)

        def dve_T(dve, name, i, dst):
            tp_full(dve, tpf_base[name] + i)
            dve.tensor_copy(dst, TP).then_inc(S("tp_read"), 1)

        PIECES = [(0, 0, 0, 128, 0), (1, 0, 130, HALF, 130), (1, 1, 0, 320, HALF)]

        def dve_residual(dve, s, r, gate):
            evac_wait(dve, s, r, 0)
            out = pj(s.f0 + r)
            for g, hh, a0, a1, c0 in PIECES:
                xs_ = x[:, r, c0:c0 + a1 - a0]
                ins = dve.scalar_tensor_tensor(xs_, out[:, hh, a0:a1], gate(r, g), xs_, MUL, ADD)
            ins.then_inc(tp_read(s, r), 1)

        def act_out_stage(act, s, norm=None):
            for r in range(s.M):
                evac_wait(act, s, r, 0)
                act_split(act, s.u0 + r + 2)
                if norm:
                    f = s.f0 + r
                    act_square(act, norm, r, x[:, r, :], (tp_read(s, r), f // 2 + 1))

        def dve_out_stage(dve, s, gate, norm=None):
            all_read(dve, s.f0)
            for r in range(s.M):
                dve_split(dve, s.u0 + r + 2)
                dve_residual(dve, s, r, gate)
                if norm and r:
                    dve_add_square(dve, norm, r - 1)
            if norm:
                dve_add_square(dve, norm, s.M - 1)

        def pe_stage(pe, s, X, ready=None):
            if ready and ready[0] == "h_ready" and s.name != "wo_ret":
                pe_first(pe, ((s, 0), (s, 1)), X, ready)
            elif ready:
                pe_first(pe, ((s, 0),), X, ready)
                pe_unit(pe, s, 1, 0, X)
            with pe.Fori(1 if ready else 0, s.M // 2) as j:
                for r in range(2):
                    pe_unit(pe, s, r, j, X)

        def act_up(act, s, l):
            cw = fconv[:, l, 2 * FIRST[s.part]:2 * (FIRST[s.part] + PARTS[s.part]), :]

            def body(r, j):
                evac_wait(act, s, r, j)
                act_split(act, s.u0 + r + 2, j)
                p = s.p0 + r // 2
                act_conv_in(act, s, r, j, cw)
                if r % 2:
                    act.wait_ge(S("cv_done"), s.c0 + r + 4 * j)
                    act.activation(t_sb[:, 0, :], t_sb[:, 0, :], ACT.Silu).then_inc(S("hid_silu"), 1)
                    act.wait_ge(S("hid_mul"), p + 1 + 2 * j)
                    act.activation(tile(hid_hi, r // 2 + 2 * j), hf2[:, 0, :], ACT.Copy).then_inc(S("hid_hi"), 1)

            for_units(act, s, body)

        def dve_up(dve, s, l):
            cw = fconv[:, l, 2 * FIRST[s.part]:2 * (FIRST[s.part] + PARTS[s.part]), :]

            def body(r, j):
                dve_split(dve, s.u0 + r + 2, j)
                dve_conv(dve, s, r, j, cw)
                if r % 2:
                    p = s.p0 + r // 2
                    dve.wait_ge(S("hid_silu"), p + 1 + 2 * j)
                    dve.wait_ge(S("cv_done"), s.c0 + r + 1 + 4 * j)
                    dve.tensor_tensor(hf2[:, 0, :], t_sb[:, 0, :], t_sb[:, 1, :], MUL).then_inc(S("hid_mul"), 1)
                    dve.wait_ge(S("hid_hi"), p + 1 + 2 * j)
                    dve.tensor_tensor(tile(hid_lo, r // 2 + 2 * j), hf2[:, 0, :],
                                      tile(hid_hi, r // 2 + 2 * j).bitcast(F32), SUB).then_inc(S("hid_ready"), 1)

            for_units(dve, s, body)

        for l in range(2):
            for n in range(3):
                stages[f"up{l}{n}"].part = n

        def dve_setup(dve):
            dve.wait_ge(S("ld_cst"), 16)
            dve.tensor_copy(ident_r[:, :], ident).then_inc(S("set"), 1)
            dve.tensor_copy(id2_r[:, :], cst[:, C_ID2:C_ID2 + 64]).then_inc(S("set"), 1)
            dve.tensor_scalar(nid2_r[:, :], cst[:, C_ID2:C_ID2 + 64], -1.0, None, MUL).then_inc(S("set"), 1)
            dve.tensor_copy(neg_r[:, :, :], cst[:, C_NEGF:C_NEGF + 256].rearrange("p (d c) -> p d c", d=2)).then_inc(S("set"), 1)
            dve.memset(cond_r[:, :, :].bitcast(F32), 0.0).then_inc(S("cond"), 1)
            dve.wait_ge(S("csil"), 1)
            dve.wait_ge(S("cond"), 1)
            dve.tensor_copy(cond_r[:, :, 0:2], csil[:, :, :]).then_inc(S("cond"), 1)
            dve.wait_ge(S("cond"), 2)
            dve.tensor_tensor(cond_r[:, :, 2:4], csil[:, :, :], cond_r[:, :, 0:2].bitcast(F32), SUB).then_inc(S("cond"), 1)

        def dve_small(dve):
            dve.wait_ge(S("ld_small"), 16 * N_SMALL)
            dve.wait_ge(S("dtp"), 1)
            dve.tensor_tensor(dtp[:, 2:3], dtp[:, 1:2], cst[:, C_SIGN:C_SIGN + 1], MUL).then_inc(S("set"), 1)
            dve.tensor_tensor(dsum[:, :], drow[:, 0, :], drow[:, 1, :], ADD).then_inc(S("set"), 1)

        def act_dt(act):
            s = stages["dt"]
            evac_wait(act, s, 0, 0)
            act_split(act, s.u0 + 2)
            act.wait_ge(S("ld_small"), 16 * N_SMALL)
            act.activation(two(da1[:, :]), pj(s.f0), ACT.Identity, bias=dtp[:, 0:1]).then_inc(tp_read(s, 0), 1)
            act.wait_ge(S("da"), 1)
            act.activation(da2[:, :], da2[:, :], ACT.Exp).then_inc(S("da_e"), 1)
            act.wait_ge(S("da_e"), 1)
            act.activation(sT[:, 0, :], da2[:, :], ACT.Ln, bias=1.0).then_inc(S("da_e"), 1)

        def dve_dt(dve):
            s = stages["dt"]
            dve_split(dve, s.u0 + 2)
            n = [0]

            def step(ins):
                n[0] += 1
                ins.then_inc(S("da"), 1)
                dve.wait_ge(S("da"), n[0])

            dve.wait_ge(tp_read(s, 0), s.f0 // 2 + 1)
            step(dve.scalar_tensor_tensor(da2[:, :], da1[:, :], -1.0, da1[:, :], MUL, MIN))
            step(dve.tensor_scalar(da1[:, :], da1[:, :], 0.0, None, MAX))
            dve.wait_ge(S("da_e"), 2)
            step(dve.tensor_scalar(sT[:, 1, :], da2[:, :], 1.0, None, ADD))
            step(dve.scalar_tensor_tensor(sT[:, 1, :], sT[:, 1, :], -1.0, da2[:, :], ADD, SUB))
            step(dve.tensor_tensor(da1[:, :], da1[:, :], sT[:, 0, :], ADD))
            step(dve.tensor_tensor(da1[:, :], da1[:, :], sT[:, 1, :], SUB))
            dve.wait_ge(S("set"), 6)
            step(dve.tensor_scalar(daT[:, :], da1[:, :], dtp[:, 2:3], None, MUL))
            assert n[0] == 7

        def pe_ssd_in(pe):
            xs_, bc, z = stages["xs"], stages["bc"], stages["z"]
            pe_first(pe, ((stages["dt"], 0),), H, hready("norm00"))
            for r in range(2):
                pe_unit(pe, xs_, r, 0, H)
            with pe.Fori(1, 4) as j:
                for r in range(2):
                    pe_unit(pe, xs_, r, j, H)
                    pe_T(pe, "xs", r - 2 + 2 * j, sT[:, r, :], (S("silu"), r - 1 + 2 * j))
            for r in range(2):
                pe_unit(pe, bc, r, 0, H)
                pe_T(pe, "xs", 6 + r, sT[:, r, :], (S("silu"), 7 + r))
            for r in range(4):
                pe_unit(pe, bc, 2 + r, 0, H)
                pe_T(pe, "b", r, bcT[:, r, :], (S("silu"), 9 + r))
            for r in range(6, 8):
                pe_unit(pe, bc, r, 0, H)
            pe_stage(pe, z, H)

        def act_ssd_in(act):
            for name in ("xs", "bc"):
                s = stages[name]
                for r in range(8):
                    c = s.c0 + r
                    evac_wait(act, s, r, 0)
                    act_split(act, s.u0 + r + 2)
                    act_conv_in(act, s, r, 0, sconv[:, c - r:c - r + 8, :])
                    if name == "xs":
                        if r >= 2:
                            act.wait_ge(S("tp_full"), tpf_base["xs"] + r - 1)
                        dst = sT[:, r % 2, :]
                    else:
                        dst = bcT[:, r, :]
                    act.wait_ge(S("cv_done"), c + 1)
                    act.activation(dst, t_sb[:, r % 2, :], ACT.Silu).then_inc(S("silu"), 1)
            s = stages["z"]
            for r in range(8):
                evac_wait(act, s, r, 0)
                act_split(act, s.u0 + r + 2)
                act.activation(two(zT[:, r, :]), pj(s.f0 + r), ACT.Silu).then_inc(tp_read(s, r), 1)

        def dve_ssd_in(dve):
            for name in ("xs", "bc"):
                s = stages[name]
                for r in range(8):
                    dve_split(dve, s.u0 + r + 2)
                    dve_conv(dve, s, r, 0, sconv[:, s.c0:s.c0 + 8, :])
                    i = s.c0 + r - 2
                    if 0 <= i < 8:
                        dve_T(dve, "xs", i, xsTM[:, :, i * 128:(i + 1) * 128])
                    elif 8 <= i < 12:
                        dve_T(dve, "b", i - 8, bTM[:, :, (i - 8) * 128:(i - 7) * 128])
            s = stages["z"]
            for r in range(8):
                dve_split(dve, s.u0 + r + 2)

        def pe_cum(pe):
            pe.wait_ge(S("da"), 7)
            pe_T(pe, "da", 0, daT[:, :], (S("da"), 7))
            pe.wait_ge(S("tp_read"), tp_base["da"] + 1)
            for c in range(NCH):
                for d in range(2):
                    pe.matmul(B6[:, c * 64 + d * 32:c * 64 + d * 32 + 32], tri[d],
                              daTM[:, c, 64 + 32 * d:96 + 32 * d], start=True, stop=True)
            pe.matmul(B7[:, 0:NCH * 64].rearrange("p (c h) -> p c h", c=NCH), ones, daTM[:, :, 64:128],
                      start=True, stop=True).then_inc(S("cum"), 1)
            tp_free(pe, tp_base["cumT"])
            for c in range(NCH):
                for d in range(2):
                    last = pe.matmul(TP[32 * d:32 * d + 32, c, :], daTM[:, c, 64 + 32 * d:96 + 32 * d], tri[d],
                                     start=True, stop=True)
            last.then_inc(S("tp_full"), 1)

        def act_cum(act):
            act.wait_ge(S("cum"), 1)
            all_read(act, stages["z"].f0 + 8)
            act.activation(ecum[:, :, :], B6[:, 0:320].rearrange("p (c h) -> p c h", c=NCH), ACT.Exp).then_inc(S("cum_e"), 1)
            act.activation(etot[:, :, :], B7[:, 0:320].rearrange("p (c h) -> p c h", c=NCH), ACT.Exp).then_inc(S("cum_e"), 1)
            act.wait_ge(S("cum_d"), 1)
            act.activation(wdt[:, :, :], wdt[:, :, :], ACT.Exp).then_inc(S("cum_e"), 1)
            tp_full(act, tpf_base["cumT"])
            act.activation(cum_r[0:64, :, :], TP[0:64, :, :], ACT.Copy).then_inc(S("cum_e"), 1)

        def dve_cum(dve):
            dve_T(dve, "da", 0, daTM[:, :, :])
            dve.wait_ge(S("cum_e"), 2)
            dve.tensor_copy(wdt[:, :, :], B7[:, 0:320].rearrange("p (c h) -> p c h", c=NCH)).then_inc(S("cum_c"), 1)
            dve.wait_ge(S("cum_c"), 1)
            dve.tensor_tensor(wdt[:, :, :], wdt[:, :, :], B6[:, 0:320].rearrange("p (c h) -> p c h", c=NCH),
                              SUB).then_inc(S("cum_d"), 1)
            dve.wait_ge(S("cum_e"), 4)
            dve.tensor_tensor(wdt[:, :, :], wdt[:, :, :], daTM[:, :, 0:64], MUL).then_inc(S("cum_d"), 1)
            dve.tensor_tensor(cum_r[64:128, :, :], TP[0:64, :, :], cum_r[0:64, :, :].bitcast(F32), SUB).then_inc(S("tp_read"), 1)

        SLOTS = ((0, 0, (0, 1)), (1, 2, (0,)), (4, 3, (1,)), (2, 4, (0, 1)), (3, 6, (0, 1)))
        SLOT = {(d, c): at + n for c, at, dirs in SLOTS for n, d in enumerate(dirs)}
        KV = [(0, 0), (1, 0), (0, 1), (0, 2), (0, 3), (1, 4), (1, 3), (1, 2)]

        def pe_ssd(pe):
            t0 = tp_base["ssd"]
            all_read(pe, stages["z"].f0 + 8)
            pe.wait_ge(S("tp_read"), t0)
            pe.wait_ge(S("cum_e"), 4)
            pe.wait_ge(S("cum_d"), 2)
            pe.wait_ge(S("set"), 4)
            pe.wait_ge(S("cond"), 3)

            def D(g, r):
                pe.wait_ge(S("ssd_E"), 2 * (4 * g + r))
                for d in range(2):
                    row = 32 * d + 4 * g + r
                    sel = id2_r[:, row:row + 1].to_broadcast([128, 128])
                    nsel = nid2_r[:, row:row + 1].to_broadcast([128, 128])
                    for c0, c1, at in ((0, 4, 512 * d), (4, 5, 1024 + 128 * d)):
                        out = flat[:, at:at + 128 * (c1 - c0)].rearrange("p (c t) -> p c t", t=128)
                        pe.matmul(out, sel, cum_r[:, c0:c1, :], start=True, stop=False)
                        pe.matmul(out, ident_r[:, :], neg_r[:, d:d + 1, :].to_broadcast([128, c1 - c0, 128]),
                                  start=False, stop=False)
                        for c in range(c0, c1):
                            last = pe.matmul(out[:, c - c0, :], cum_r[:, c, :], nsel, start=False, stop=(c == c1 - 1))
                last.then_inc(S("ssd_D"), 1)

            cols = list(range(MA // 4, 24))

            def some_cols(m):
                while cols and 4 * cols[0] + 3 < MA + m:
                    pe_mod_cols(pe, cols.pop(0))

            def group(g):
                tp_free(pe, t0 + 3 * g)
                for c in range(NCH):
                    last = pe.matmul(TP[:, c, :], tile(bcT, g)[:, chunk(c)], tile(bcT, SG + g)[:, chunk(c)],
                                     start=True, stop=True)
                last.then_inc(S("tp_full"), 1)
                D(g, 0)
                for r in range(SR):
                    h = 4 * g + r
                    if r < SR - 1:
                        D(g, r + 1)
                    pe_mod_unit(pe, MA + 5 * h)
                    pe.wait_ge(S("ssd_in"), h)
                    pe.wait_ge(S("ssd_v"), 4 * h + 4)
                    for c, at, dirs in SLOTS:
                        last = pe.matmul(B6[:, at * 64:(at + len(dirs)) * 64].rearrange("p (d v) -> p d v", v=64),
                                         bTM[:, c, g * 128:(g + 1) * 128],
                                         xv[:, r % 2, 2 + dirs[0]:2 + dirs[-1] + 1, c, :], start=True, stop=True)
                    last.then_inc(S("ssd_kv"), 1)
                    pe_mod_unit(pe, MA + 5 * h + 1)
                    pe.wait_ge(S("ssd_pt"), 2 * h + 2)
                    pe.wait_ge(S("ssd_yr"), h)
                    some_cols(5 * h)
                    for c in range(NCH):
                        for d in range(2):
                            last = pe.matmul(B7[:, c * 64:(c + 1) * 64], E[:, d, c, :], xv[:, r % 2, d, c, :],
                                             start=(d == 0), stop=(d == 1))
                    last.then_inc(S("ssd_y"), 1)
                    pe_mod_unit(pe, MA + 5 * h + 2)
                    pe.wait_ge(S("ssd_rec"), 8 * h + 8)
                    for c in range(1, NCH):
                        last = pe.matmul(B6[:, (c - 1) * 128:c * 128], tile(bcT, SG + g)[:, chunk(c)],
                                         Sst[:, r % 2, c - 1, :, :].rearrange("p d v -> p (d v)"), start=True, stop=True)
                    last.then_inc(S("ssd_i"), 1)
                    pe_mod_unit(pe, MA + 5 * h + 3)
                    pe_mod_unit(pe, MA + 5 * h + 4)
                    if r % 2:
                        q = r // 2
                        pe.wait_ge(S("ssd_yt"), h + 1)
                        tp_free(pe, t0 + 3 * g + 1 + q)
                        for c in range(NCH):
                            last = pe.transpose(TP[:, c, :], yb[:, q, c, :], ident)
                        last.then_inc(S("tp_full"), 1)

            for g in range(SG):
                group(g)
                pe.wait_ge(S("ssd_yr"), 4 * g + 4)
                some_cols(20 * g + 20)

        def act_ssd(act):
            t0, f0 = tp_base["ssd"], tpf_base["ssd"]
            with act.Fori(0, SG) as g:
                tp_full(act, f0 + 3 * g)
                act.activation(GT[:, :, :], TP, ACT.Copy).then_inc(S("tp_read"), 1)

                def exps(r):
                    h = 4 * g + r
                    act.wait_ge(S("ssd_D"), h + 1)
                    if r:
                        act.wait_ge(S("ssd_y"), h)
                    act.activation(E[:, :, 0:4, :].rearrange("p d c t -> p d (c t)"),
                                   flat[:, 0:1024].rearrange("p (d c) -> p d c", d=2), ACT.Exp).then_inc(S("ssd_E"), 1)
                    act.activation(E[:, :, 4, :], flat[:, 1024:1280].rearrange("p (d c) -> p d c", d=2),
                                   ACT.Exp).then_inc(S("ssd_E"), 1)

                exps(0)
                for r in range(SR):
                    for n in range(5):
                        if n == 2 and r + 1 < SR:
                            exps(r + 1)
                        act_modB(act, 5 * r + n, g)

        def dve_ssd(dve):
            t0, f0 = tp_base["ssd"], tpf_base["ssd"]
            dve.wait_ge(S("ld_s0"), 16)
            dve.wait_ge(S("cum_d"), 2)
            with dve.Fori(0, SG) as g:
                for r in range(SR):
                    h = 4 * g + r

                    def mod(n):
                        dve_split(dve, stages["modB"].u0 + 5 * r + n + 2, 5 * g)

                    def row(t, d, c0=0, c1=NCH, w=64):
                        return t[:, c0:c1, ds(4 * g + r + 32 * d, 1)].to_broadcast([128, c1 - c0, w])

                    xh = xsTM[:, :, ds(h * 64, 64)]
                    if r >= 2:
                        dve.wait_ge(S("ssd_i"), h - 1)
                    for k, (t, d) in enumerate(((daTM, 0), (daTM, 1), (wdt, 0), (wdt, 1))):
                        dve.tensor_tensor(xv[:, r % 2, k, :, :], xh, row(t, d), MUL).then_inc(S("ssd_v"), 1)
                    dve.wait_ge(S("ssd_E"), 2 * h + 2)
                    for d in range(2):
                        dve.tensor_tensor(E[:, d, :, :], E[:, d, :, :], GT[:, :, :], MUL).then_inc(S("ssd_pt"), 1)
                    mod(0)
                    dve.wait_ge(S("ssd_kv"), h + 1)
                    dve.tensor_copy(sout[:, :, ds(h, 1), :].rearrange("p d a c -> p d (a c)"),
                                    B6[:, 0:128].rearrange("p (d c) -> p d c", d=2)).then_inc(S("ssd_so"), 1)
                    for d in range(2):
                        dve.tensor_copy(Sst[:, r % 2, 3 * d, d, :],
                                        s0[:, d, ds(h, 1), :].rearrange("p a c -> p (a c)")).then_inc(S("ssd_rec"), 1)
                    for k in range(3):
                        for d in range(2):
                            c, to = (k + 1, k + 2) if d == 0 else (4 - k, 3 - k)
                            dve.wait_ge(S("ssd_rec"), 8 * h + 2 * k + d + 1)
                            dve.scalar_tensor_tensor(
                                Sst[:, r % 2, to - 1, d, :], Sst[:, r % 2, c - 1, d, :],
                                etot[:, c, ds(4 * g + r + 32 * d, 1)],
                                B6[:, SLOT[d, c] * 64:(SLOT[d, c] + 1) * 64], MUL, ADD).then_inc(S("ssd_rec"), 1)
                    mod(1)
                    yh = yb[:, r // 2, :, (r % 2) * 64:(r % 2) * 64 + 64]
                    dve.wait_ge(S("ssd_y"), h + 1)
                    if r % 2 == 0:
                        dve.wait_ge(S("tp_full"), f0 + 3 * g)
                    dve.scalar_tensor_tensor(yh, xh, dsum[:, ds(h, 1)], B7[:, 0:320].rearrange("p (c v) -> p c v", c=NCH),
                                             MUL, ADD).then_inc(S("ssd_yr"), 1)
                    mod(2)
                    dve.wait_ge(S("ssd_i"), h + 1)
                    for d in range(2):
                        ins = dve.tensor_tensor(inter[:, d, :, :], B6.rearrange("p (c d v) -> p d c v", c=4, d=2)[:, d, :, :],
                                                row(ecum, d, 1, 5), MUL)
                    ins.then_inc(S("ssd_in"), 1)
                    dve.wait_ge(S("ssd_yr"), h + 1)
                    dve.wait_ge(S("ssd_in"), h + 1)
                    dve.tensor_tensor(yh[:, 1:5, :], yh[:, 1:5, :], inter[:, 0, :, :], ADD).then_inc(S("ssd_ya"), 1)
                    dve.wait_ge(S("ssd_ya"), h + 1)
                    dve.tensor_tensor(yh[:, 1:5, :], yh[:, 1:5, :], inter[:, 1, :, :], ADD).then_inc(S("ssd_yt"), 1)
                    mod(3)
                    mod(4)
                    if r % 2:
                        q = r // 2
                        tp_full(dve, f0 + 3 * g + 1 + q)
                        zt = zT[:, ds(2 * g + q, 1), :].rearrange("p a c -> p (a c)")
                        dve.tensor_tensor(zt[:, 0:128], zt[:, 0:128], TP[:, 0, :], MUL)
                        zs = zt[:, 130:642].rearrange("p (c t) -> p c t", c=4)
                        dve.tensor_tensor(zs, zs, TP[:, 1:5, :], MUL).then_inc(S("tp_read"), 1)

        def pe_ret_in(pe):
            qk, v, g_ = stages["qk"], stages["v"], stages["g"]
            pe_first(pe, ((qk, 0), (qk, 1)), H, hready("again"))
            for r in range(2, 6):
                pe_unit(pe, qk, r, 0, H)
            for r in range(6, 8):
                pe_unit(pe, qk, r, 0, H)
                f = qk.f0 + r - 2
                pe_T(pe, "k", r - 6, qkT[:, r - 2, :], (S(f"pj_read{f % 2}"), f // 2 + 1))
            for r in range(2):
                pe_unit(pe, v, r, 0, H)
                f = qk.f0 + 6 + r
                pe_T(pe, "k", 2 + r, qkT[:, 6 + r, :], (S(f"pj_read{f % 2}"), f // 2 + 1))
            with pe.Fori(1, 4) as j:
                for r in range(2):
                    pe_unit(pe, v, r, j, H)
                    f = v.f0 + r
                    pe_T(pe, "v", r - 2 + 2 * j, sT2[:, r, :], (S(f"pj_read{f % 2}"), f // 2 + j))
            for r in range(2):
                pe_unit(pe, g_, r, 0, H)
                f = v.f0 + 6 + r
                pe_T(pe, "v", 6 + r, sT2[:, r, :], (S(f"pj_read{f % 2}"), f // 2 + 1))
            with pe.Fori(1, 4) as j:
                for r in range(2):
                    pe_unit(pe, g_, r, j, H)

        def act_ret_in(act):
            for name in ("qk", "v", "g"):
                s = stages[name]
                for r in range(8):
                    evac_wait(act, s, r, 0)
                    act_split(act, s.u0 + r + 2)
                    src = pj(s.f0 + r)
                    if name == "qk":
                        ins = act.activation(two(qkT[:, r, :]), src, ACT.Copy, scale=RDK ** -0.5 if r >= 4 else 1.0)
                    elif name == "v":
                        if r >= 2:
                            act.wait_ge(S("tp_full"), tpf_base["v"] + r - 1)
                        ins = act.activation(two(sT2[:, r % 2, :]), src, ACT.Copy)
                    else:
                        ins = act.activation(two(gT[:, r, :]), src, ACT.Silu)
                    ins.then_inc(tp_read(s, r), 1)
                    if name == "g" and r >= 2:
                        act_square(act, "normS", r - 2, zT[:, r - 2, :])
            for k in range(KT - 2, KT):
                act_square(act, "normS", k, zT[:, k, :])

        def dve_ret_in(dve):
            for n, name in enumerate(("qk", "v", "g")):
                s = stages[name]
                for r in range(8):
                    dve_split(dve, s.u0 + r + 2)
                    i = 8 * n + r - 6
                    if 0 <= i < 4:
                        dve_T(dve, "k", i, kTM[:, :, i * 128:(i + 1) * 128])
                    elif 4 <= i < 12:
                        dve_T(dve, "v", i - 4, vTM[:, :, (i - 4) * 128:(i - 3) * 128])
                    if name == "g" and r >= 2:
                        dve_add_square(dve, "normS", r - 2)
            for k in range(KT - 2, KT):
                dve_add_square(dve, "normS", k)

        def act_ret_setup(act):
            act.wait_ge(S("pe_unit"), stages["wo_ssm"].u0 + 8)
            for d, (m, at) in enumerate(((mTf, C_IJF), (mTb, C_IJB))):
                for h in range(RH):
                    last = act.activation(m[:, h, :], cst[:, at:at + 128], ACT.Exp, scale=lrow[:, d * 8 + h:d * 8 + h + 1])
            last.then_inc(S("ret_set"), 1)
            for n in range(4):
                last = act.activation(rdec[:, n, :], lrow[:, :], ACT.Exp, scale=cst[:, C_RPOS + n:C_RPOS + n + 1])
            act.activation(rtot[:, :, :], lpair[:, :, :], ACT.Exp, scale=128.0).then_inc(S("ret_set"), 1)

        def dve_ret_setup(dve):
            dve.wait_ge(S("ret_set"), 1)
            for d, m in enumerate((mTf, mTb)):
                dve.tensor_tensor(m[:, :, :], m[:, :, :], tri[d].unsqueeze(1).to_broadcast([128, RH, 128]),
                                  MUL).then_inc(S("ret_m"), 1)
            dve.wait_ge(S("ret_m"), 2)
            dve.tensor_tensor(mTf[:, :, :], mTf[:, :, :], mTb[:, :, :], ADD).then_inc(S("ret_m"), 1)

        def pe_ret(pe):
            all_read(pe, stages["wo_ssm"].f0 + 8)
            pe.wait_ge(S("tp_read"), tp_base["normS"] + 1)
            for p in range(4):
                if p:
                    pe.wait_ge(S("ret_rd"), 4 * p)
                for e in range(2):
                    rows = slice(64 * e, 64 * e + 64)
                    out = flat[:, 1024 * e:1024 * e + 640].rearrange("p (c t) -> p c t", c=NCH)
                    for c in range(NCH):
                        last = pe.matmul(out[:, c, :], tile(qkT, 4 + p)[rows, chunk(c)], tile(qkT, p)[rows, chunk(c)],
                                         start=True, stop=True)
                    last.then_inc(S("ret_s"), 1)
                pe.wait_ge(S("ret_kw"), 4 * p + 4)
                for n, (d, c) in enumerate(KV):
                    for e in range(2):
                        last = pe.matmul(flat[64 * e:64 * e + 64, 2048 + n * 128:2048 + (n + 1) * 128],
                                         kw[:, d, c, 64 * e:64 * e + 64], vTM[:, c, ds(p * 256 + 128 * e, 128)],
                                         start=True, stop=True)
                last.then_inc(S("ret_kv"), 1)
                for e in range(2):
                    rows = slice(64 * e, 64 * e + 64)
                    pe.wait_ge(S("ret_pt"), 2 * p + e + 1)
                    out = flat[:, 1024 * e:1024 * e + 640].rearrange("p (c t) -> p c t", c=NCH)
                    for c in range(NCH):
                        last = pe.matmul(out[:, c, :], PTr[:, e, c, :], vTM[:, c, ds(p * 256 + 128 * e, 128)],
                                         start=True, stop=True)
                    last.then_inc(S("ret_y"), 1)
                    if e == 0:
                        pe.wait_ge(S("ret_rec"), 8 * p + 8)
                    else:
                        pe.wait_ge(S("ret_rd"), 4 * p + 2)
                    for c in range(1, NCH):
                        last = pe.matmul(flat[:, 3072 + (c - 1) * 256:3072 + c * 256], tile(qkT, p)[rows, chunk(c)],
                                         Sr[rows, c - 1, :, :].rearrange("p d v -> p (d v)"), start=True, stop=True)
                    last.then_inc(S("ret_i"), 1)

        def act_ret(act):
            act.wait_ge(S("tp_read"), tp_base["v"] + 8)
            act.wait_ge(S("ret_set"), 2)
            act.wait_ge(S("h_ready"), KT * (APPLIED.index("normS") + 1))
            with act.Fori(0, 4) as p:
                for d in range(2):
                    for e in range(2):
                        act.activation(kw[:, d, :, 64 * e:64 * e + 64], kTM[:, :, ds(p * 128 + 64 * e, 64)], ACT.Copy,
                                       scale=rdec[:, 2 + d, ds(2 * p + e + 8 * d, 1)]).then_inc(S("ret_kw"), 1)
                for e in range(2):
                    act.wait_ge(S("ret_y"), 2 * p + e + 1)
                    act.activation(yret[:, :, ds(p * 256 + e * 128, 128)],
                                   flat[:, 1024 * e:1024 * e + 640].rearrange("p (c t) -> p c t", c=NCH),
                                   ACT.Copy).then_inc(S("ret_yc"), 1)

        def dve_ret(dve):
            dve.wait_ge(S("ret_m"), 3)
            dve.wait_ge(S("ld_s0r"), 16)
            with dve.Fori(0, 4) as p:
                for e in range(2):
                    dve.wait_ge(S("ret_s"), 2 * p + e + 1)
                    dve.tensor_tensor(PTr[:, e, :, :], flat[:, 1024 * e:1024 * e + 640].rearrange("p (c t) -> p c t", c=NCH),
                                      mTf[:, ds(2 * p + e, 1), :].to_broadcast([128, NCH, 128]), MUL).then_inc(S("ret_pt"), 1)
                dve.wait_ge(S("ret_kv"), p + 1)
                kv = flat[:, 2048:3072].rearrange("p (n v) -> p n v", n=8)
                dve.tensor_copy(soutr[:, :, ds(p, 1), :].rearrange("p d a v -> p d (a v)"), kv[:, 0:2, :]).then_inc(S("ret_so"), 1)
                for d in range(2):
                    dve.tensor_copy(Sr[:, 3 * d, d, :], s0r[:, ds(p, 1), d, :].rearrange("p a v -> p (a v)")).then_inc(S("ret_rec"), 1)
                for k in range(3):
                    for d in range(2):
                        dst = k + 1 if d == 0 else 2 - k
                        dve.wait_ge(S("ret_rec"), 8 * p + 2 * k + d + 1)
                        ins = dve.scalar_tensor_tensor(Sr[:, dst, d, :], Sr[:, dst - 1 if d == 0 else dst + 1, d, :],
                                                       rtot[:, d, ds(p, 1)], kv[:, 2 + 3 * d + k, :], MUL, ADD)
                        ins.then_inc(S("ret_rec"), 1)
                for e in range(2):
                    yh = yret[:, 1:5, ds(p * 256 + e * 128, 128)]
                    dve.wait_ge(S("ret_yc"), 2 * p + e + 1)
                    dve.wait_ge(S("ret_i"), 2 * p + e + 1)
                    it = flat[:, 3072:4096].rearrange("p (c d v) -> p d c v", c=4, d=2)
                    for d in range(2):
                        if d:
                            dve.wait_ge(S("ret_rd"), 4 * p + 2 * e + 1)
                        dve.scalar_tensor_tensor(yh, it[:, d, :, :], rdec[:, d, ds(2 * p + e + 8 * d, 1)], yh,
                                                 MUL, ADD).then_inc(S("ret_rd"), 1)
                    dve.wait_ge(S("ret_rd"), 4 * p + 2 * e + 2)
                    for c in range(NCH):
                        ins = dve.bn_stats(bst[:, ds(2 * p + e, 1), c, :].rearrange("p a b -> p (a b)"),
                                           yret[:, c, ds(p * 256 + e * 128, 128)])
                    ins.then_inc(S("ret_bn"), 1)
            dve.wait_ge(S("ret_bn"), RH)
            for h in range(RH):
                for c in range(NCH):
                    ins = dve.bn_aggr(mv[:, h, c, :], bst[:, h, c, :])
            ins.then_inc(S("ret_ag"), 1)

        def act_ret_out(act):
            act.wait_ge(S("ret_ag"), 1)
            act.activation(rsd[:, :, :], mv[:, :, :, 1], ACT.Sqrt, bias=eps).then_inc(S("ret_sq"), 1)
            n0 = KT * APPLIED.index("retT")
            for k in range(KT):
                act.wait_ge(S("tp_read"), tp_base["retT"] + k + 1)
                act.activation(h_hi[:, k, :], gT[:, k, :], ACT.Copy).then_inc(S("h_hi"), 1)

        def dve_ret_out(dve):
            dve.wait_ge(S("ret_sq"), 1)
            dve.reciprocal(rsd[:, :, :], rsd[:, :, :]).then_inc(S("ret_rc"), 1)
            dve.wait_ge(S("ret_rc"), 1)
            n0 = KT * APPLIED.index("retT")
            for k in range(KT + 2):
                if k < KT:
                    for c in range(NCH):
                        yc = yret[:, c, k * 128:(k + 1) * 128]
                        ins = dve.tensor_scalar(yc, yc, mv[:, k, c, 0:1], rsd[:, k, c:c + 1], SUB, MUL)
                    ins.then_inc(S("ret_nrm"), 1)
                if 1 <= k <= KT:
                    tp_full(dve, tpf_base["retT"] + k - 1)
                    for (c0, c1), at in GROUPS:
                        g_ = gT[:, k - 1, c0:c1]
                        ins = dve.scalar_tensor_tensor(g_, flat[:, 2048 + at:2048 + at + c1 - c0], gngain[:, k - 1:k], g_, MUL, MUL)
                    ins.then_inc(S("tp_read"), 1)
                if k >= 2:
                    dve.wait_ge(S("h_hi"), n0 + k - 1)
                    dve.tensor_tensor(h_lo[:, k - 2, :], gT[:, k - 2, :], h_hi[:, k - 2, :].bitcast(F32), SUB).then_inc(S("h_ready"), 1)

        def pe_ret_out(pe):
            for k in range(KT):
                pe.wait_ge(S("ret_nrm"), k + 1)
                tp_free(pe, tp_base["retT"] + k)
                for c in range(NCH):
                    last = pe.transpose(TP[:, c, :], yret[:, c, k * 128:(k + 1) * 128], ident)
                last.then_inc(S("tp_full"), 1)

        def pe_qkv(pe):
            s = stages["qkv"]
            ready = lambda r, k: (S(f"pj_read{(s.f0 + r) % 2}"), (s.f0 + r) // 2 + 1 + k)
            pe_first(pe, ((s, 0), (s, 1)), H, hready("norm10"))
            with pe.Fori(1, s.M // 2) as j:
                for r in range(2):
                    pe_unit(pe, s, r, j, H)
                    pe_T(pe, "qkv", r - 2 + 2 * j, sT3[:, r, :], ready(r, j - 1))
            for r in range(2):
                pe_T(pe, "qkv", s.M - 2 + r, sT3[:, r, :], ready(s.M - 2 + r, 0))

        def act_qkv(act):
            s = stages["qkv"]

            def body(r, j):
                evac_wait(act, s, r, j)
                act_split(act, s.u0 + r + 2, j)
                if not (isinstance(j, int) and r < 2):
                    act.wait_ge(S("tp_full"), tpf_base["qkv"] + r - 1 + 4 * j)
                act.activation(two(sT3[:, r % 2, :]), pj(s.f0 + r), ACT.Copy).then_inc(tp_read(s, r), 1)

            for_units(act, s, body, peel=1)

        def dve_qkv(dve):
            s = stages["qkv"]

            def put(i):
                tp_full(dve, tpf_base["qkv"] + i)
                dst = qkv[:, :, i * 128:(i + 1) * 128] if isinstance(i, int) else qkv[:, :, ds(i * 128, 128)]
                dve.tensor_copy(dst, TP).then_inc(S("tp_read"), 1)

            def body(r, j):
                dve_split(dve, s.u0 + r + 2, j)
                if not (isinstance(j, int) and r < 2):
                    put(r - 2 + 4 * j)

            for_units(dve, s, body, peel=1)
            for i in range(s.M - 2, s.M):
                put(i)

        QK = (AH + AG) * AD

        def act_qk(act):
            act.wait_ge(S("tp_read"), tp_base["qkv"] + 12)
            for c in range(NCH):
                if c:
                    act.wait_ge(S("at_red"), c)
                act.activation(rt1[:, :], qkv[:, c, 0:QK], ACT.Square).then_inc(S("at_sq"), 1)
            act.wait_ge(S("at_red"), NCH)
            act.activation(astat[:, 1, :, :], astat[:, 0, :, :], ACT.Sqrt, bias=eps, scale=1.0 / AD).then_inc(S("at_sq"), 1)

        def dve_qk(dve):
            n = [0]

            def step(ins):
                n[0] += 1
                ins.then_inc(S("at_v"), 1)
                dve.wait_ge(S("at_v"), n[0])

            for c in range(NCH):
                dve.wait_ge(S("at_sq"), c + 1)
                dve.tensor_reduce(astat[:, 0, c, :], rt1[:, :].rearrange("p (h d) -> p h d", d=AD), AX.X, ADD).then_inc(S("at_red"), 1)
            dve.wait_ge(S("at_sq"), NCH + 1)
            step(dve.reciprocal(astat[:, 2, :, :], astat[:, 1, :, :]))
            for c in range(NCH):
                xc = qkv[:, c, 0:QK].rearrange("p (h d) -> p h d", d=AD)
                step(dve.tensor_tensor(xc, xc, astat[:, 2, c, :].unsqueeze(2).to_broadcast([128, AH + AG, AD]), MUL))
                for g, (h0, h1) in enumerate(((0, AH), (AH, AH + AG))):
                    ins = dve.tensor_tensor(xc[:, h0:h1, :], xc[:, h0:h1, :],
                                            qkgain[:, g:g + 1, :].to_broadcast([128, h1 - h0, AD]), MUL)
                step(ins)
                if c == 0:
                    continue
                dve.wait_ge(S("ld_rope"), 16)
                cos, sin = rope[:, 0, c - 1, :], rope[:, 1, c - 1, :]
                dve.tensor_tensor(rt1[:, :].rearrange("p (h d) -> p h d", d=AD), xc,
                                  cos.unsqueeze(1).to_broadcast([128, AH + AG, AD]), MUL)
                x5 = qkv[:, c, 0:QK].rearrange("p (h a b f) -> p h a b f", a=2, b=2, f=16)
                r5 = rt2[:, :].rearrange("p (h a b f) -> p h a b f", a=2, b=2, f=16)
                s4 = sin.rearrange("p (a b f) -> p a b f", a=2, b=2)
                for b in range(2):
                    ins = dve.tensor_tensor(r5[:, :, :, b, :], x5[:, :, :, 1 - b, :],
                                            s4[:, :, b, :].unsqueeze(1).to_broadcast([128, AH + AG, 2, 16]), MUL)
                step(ins)
                step(dve.tensor_tensor(qkv[:, c, 0:QK], rt1[:, :], rt2[:, :], ADD))
            assert n[0] == 1 + 2 * NCH + 2 * (NCH - 1)
        ROPED = 1 + 2 * NCH + 2 * (NCH - 1)

        def pe_qkT(pe):
            for c in range(NCH):
                pe.wait_ge(S("at_v"), 3 + 4 * c)
                tp_free(pe, tp_base["qkT"] + c)
                for m in range(8):
                    pe.transpose(QKT[:, m, :], qkv[:, c, m * 128:(m + 1) * 128], ident)
                for g in range(AG):
                    at = (AH + g) * AD
                    for half in range(2):
                        last = pe.matmul(B6[64 * half:64 * half + 64, g * 128:(g + 1) * 128], qkv[:, c, at:at + AD],
                                         ident, start=True, stop=True)
                last.then_inc(S("tp_full"), 1)

        QKT = flat[:, 2048:3072].rearrange("p (m t) -> p m t", m=8)

        def act_qkT(act):
            for c in range(NCH):
                tp_full(act, tpf_base["qkT"] + c)
                act.activation(qT[:, :, chunk(c)], QKT, ACT.Copy, scale=AD ** -0.5)
                act.activation(kT[:, :, c + 1 if c else 0, :], B6.rearrange("p (g t) -> p g t", g=AG),
                               ACT.Copy).then_inc(S("tp_read"), 1)

        NG = NCH * AR
        CHUNKS = (1, 2, 3, 4, 0)
        PART_OF = ((0, 2), (2, 3), (3, 4), (4, 5))

        def place(n):
            return n // AR, CHUNKS[n // AR], n % AR

        def blocks(c):
            return (0, 1) if c == 0 else (1, 6)

        def width(c):
            return 128 * (blocks(c)[1] - blocks(c)[0])

        def pe_att(pe):
            t0 = tp_base["att"]
            pe.wait_ge(S("tp_read"), t0)
            pe.wait_ge(S("ld_past"), 32)
            all_read(pe, stages["qkv"].f0 + 12)

            for g in range(AG):
                def scores(n):
                    k, c, r = place(n)
                    rows, (b0, b1) = slice(64 * (r % 2), 64 * (r % 2) + 64), blocks(c)
                    pe.wait_ge(S("at_e"), NG * g + (n - 1 if n >= 2 else 0))
                    q = tile(qT, 2 * g + r // 2)[rows, chunk(c)]
                    o0 = 1024 * (n % 2)
                    for c0, c1 in ((b0, min(b1, b0 + 4)), (b0 + 4, b1)):
                        if c0 < c1:
                            last = pe.matmul(flat[:, o0 + (c0 - b0) * 128:o0 + (c1 - b0) * 128], q,
                                             kT[rows, g, c0:c1, :], start=True, stop=True)
                    last.then_inc(S("at_s"), 1)

                def trans(n):
                    k, c, r = place(n)
                    pe.wait_ge(S("at_p"), NG * g + n + 1)
                    tp_free(pe, t0 + NG * g + n)
                    for b in range(blocks(c)[1] - blocks(c)[0]):
                        last = pe.transpose(TP[:, b, :], Pr[:, n % 2, b * 128:(b + 1) * 128], ident)
                    last.then_inc(S("tp_full"), 1)

                def values(k, part):
                    c = CHUNKS[k]
                    b0, b1 = blocks(c)
                    p0, p1 = PART_OF[part]
                    if p0 == 0:
                        pe.wait_ge(S("tp_read"), t0 + NG * g + AR * k + AR)
                        pe.wait_ge(S("at_lo"), NCH * g + (k - 1 if k >= 2 else 0))
                    for b in range(b0 + p0, min(b0 + p1, b1)):
                        at = (AH + AG) * AD + g * AD
                        v = vpast[:, g * AD:(g + 1) * AD] if b == 1 else qkv[:, max(b - 1, 0), at:at + AD]
                        for par in range(2):
                            last = pe.matmul((B6, B7)[k % 2][64 * par:64 * par + 64, 0:256].rearrange("p (m t) -> p m t", m=2), v,
                                             PT[:, k % 2, b - b0, par:AR:2, :], start=(b == b0), stop=(b == b1 - 1))
                        if b == b1 - 1:
                            last.then_inc(S("at_o"), 1)

                scores(0)
                for n in range(NG):
                    if n + 1 < NG:
                        scores(n + 1)
                    if n >= AR:
                        values(n // AR - 1, n % AR)
                    trans(n)
                values(NCH - 1, 0)

        def act_att(act):
            t0, f0 = tp_base["att"], tpf_base["att"]
            with act.Fori(0, AG) as g:
                def probs(n):
                    k, c, r = place(n)
                    act.wait_ge(S("tp_full"), f0 + NG * g + (n - 1 if n >= 2 else 0))
                    act.wait_ge(S("at_m"), NG * g + n + 1)
                    act.activation(Pr[:, n % 2, 0:width(c)], flat[:, 1024 * (n % 2):1024 * (n % 2) + width(c)], ACT.Exp,
                                   bias=amax[:, n % 2, 0:1], accum_out=asum[:, n % 2, 0:1]).then_inc(S("at_e"), 1)

                def put(n):
                    k, c, r = place(n)
                    nb = blocks(c)[1] - blocks(c)[0]
                    tp_full(act, f0 + NG * g + n)
                    if k >= 2:
                        act.wait_ge(S("at_o"), NCH * g + k - 1)
                    act.activation(PT[:, k % 2, 0:nb, r, :], TP[:, 0:nb, :], ACT.Copy).then_inc(S("tp_read"), 1)

                def out(k):
                    act.wait_ge(S("at_o"), NCH * g + k + 1)
                    act.activation(h_hi[:, ds(2 * g, 2), chunk(CHUNKS[k])], (B6, B7)[k % 2][:, 0:256].rearrange("p (m t) -> p m t", m=2),
                                   ACT.Copy).then_inc(S("at_hi"), 1)

                probs(0)
                for n in range(NG):
                    if n + 1 < NG:
                        probs(n + 1)
                    put(n)
                    if n >= 2 * AR and n % AR == 0:
                        out(n // AR - 2)
                for k in range(NCH - 2, NCH):
                    out(k)

        def dve_att(dve):
            dve.wait_ge(S("at_v"), ROPED)
            for h in H:
                for at in EMPTY:
                    ins = dve.memset(h[:, :, at:at + 2].bitcast(F32), 0.0)
            ins.then_inc(S("at_empty"), 1)
            with dve.Fori(0, AG) as g:
                def top(n):
                    k, c, r = place(n)
                    dve.wait_ge(S("at_s"), NG * g + n + 1)
                    dve.tensor_reduce(amax[:, n % 2, 0:1], flat[:, 1024 * (n % 2):1024 * (n % 2) + width(c)], AX.X, MAX,
                                      negate=True).then_inc(S("at_m"), 1)

                def norm(n):
                    k, c, r = place(n)
                    w = width(c)
                    dve.wait_ge(S("at_e"), NG * g + n + 1)
                    dve.reciprocal(asum[:, n % 2, 1:2], asum[:, n % 2, 0:1]).then_inc(S("at_r"), 1)
                    dve.wait_ge(S("at_r"), NG * g + n + 1)
                    dve.tensor_scalar(Pr[:, n % 2, 0:w], Pr[:, n % 2, 0:w], asum[:, n % 2, 1:2], None, MUL).then_inc(S("at_p"), 1)

                def out(k):
                    dve.wait_ge(S("at_hi"), NCH * g + k + 1)
                    dve.tensor_tensor(h_lo[:, ds(2 * g, 2), chunk(CHUNKS[k])], (B6, B7)[k % 2][:, 0:256].rearrange("p (m t) -> p m t", m=2),
                                      h_hi[:, ds(2 * g, 2), chunk(CHUNKS[k])].bitcast(F32), SUB).then_inc(S("at_lo"), 1)

                top(0)
                for n in range(NG):
                    norm(n)
                    if n + 1 < NG:
                        top(n + 1)
                    if n >= 2 * AR and n % AR == 0:
                        out(n // AR - 2)
                for k in range(NCH - 2, NCH):
                    out(k)

        def gate(l, part):
            return lambda k, g: modcol(l, part, k, g)

        def gain(l, w):
            return lambda k, g: gains[:, l, w, k, g:g + 1]

        N_SMALL = 12
        block = ctx.enter_context(nc.Block())

        @block.sync
        def _(sp):
            sp.dma_start(cond[:, :, :], a["cond"]).then_inc(S("ld_cond"), 16)
            sp.dma_start(cst[:, :], a["consts"]).then_inc(S("ld_cst"), 16)
            sp.dma_start(x[:, :, :], a["x"]).then_inc(S("ld_small"), 16)
            for t, src in ((bmod[:, :, :], "b_mod"), (norms[:, :, :, :], "norms"), (ssmgain[:, :], "ssm_gain"),
                           (gngain[:, :], "gn_gain"), (fconv[:, :, :, :], "ffn_conv"), (sconv[:, :, :], "ssm_conv"),
                           (dtp[:, 0:2], "dt_params"), (lpair[:, :, :], "decay_pair")):
                sp.dma_start(t, a[src]).then_inc(S("ld_small"), 16)
            sp.dma_start(lrow[:, :], a["decay"].partition_broadcast(128)).then_inc(S("ld_small"), 16)
            sp.dma_start(drow[:, :, :], a["ssm_d"].partition_broadcast(128)).then_inc(S("ld_small"), 16)
            sp.dma_start(qkgain[:, :, :], a["qk_gain"].partition_broadcast(128)).then_inc(S("ld_small"), 16)
            for s in order:
                if s.name == "qkv":
                    sp.wait_ge(S("h_ready"), KT * (APPLIED.index("retT") + 1))
                    sp.dma_start(kT[:, :, 1, :], a["k_past"]).then_inc(S("ld_past"), 16)
                    sp.dma_start(vpast[:, :], a["v_past"]).then_inc(S("ld_past"), 16)
                if s.M // 4 >= 2:
                    for r in range(4):
                        sp_unit(sp, s, r, 0)
                    with sp.Fori(1, s.M // 4) as j:
                        for r in range(4):
                            sp_unit(sp, s, r, j)
                    rest = s.M // 4 * 4
                else:
                    rest = 0
                for r in range(rest, s.M):
                    sp_unit(sp, s, r, 0)
            all_read(sp, order[-1].f0 + 8)
            sp.dma_start(o["y"], x[:, :, :]).then_inc(S("st_y"), 16)
            sp.wait_ge(S("st_y"), 16)

        @block.scalar
        def _(act):
            act.wait_ge(S("ld_cond"), 16)
            act.activation(csil[:, :, :], cond[:, :, :], ACT.Silu).then_inc(S("csil"), 1)
            act.wait_ge(S("ld_cst"), 16)
            act.wait_ge(S("ld_small"), 16 * N_SMALL)
            act.activation(dtp[:, 1:2], dtp[:, 1:2], ACT.Exp).then_inc(S("dtp"), 1)
            for k in range(KT):
                act_square(act, "norm00", k, x[:, k, :])
            act_root(act, "norm00")
            act_split(act, 0)
            act_split(act, 1)
            act_modA(act)
            act_apply(act, "norm00", gate(0, 0))
            act_dt(act)
            act_ssd_in(act)
            act.wait_ge(S("pe_unit"), stages["z"].u0 + 8)
            act.dma_start(s0[:, :, :, :], a["s_ssm"]).then_inc(S("ld_s0"), 16)
            act_cum(act)
            act_ssd(act)
            act.wait_ge(S("ssd_so"), SH)
            act.dma_start(o["s_ssm"], sout[:, :, :, :]).then_inc(S("st_ssm"), 16)
            act.wait_ge(S("st_ssm"), 16)
            act_apply(act, "again", gate(0, 0))
            act_ret_in(act)
            act_root(act, "normS")
            act_apply(act, "normS")
            act_out_stage(act, stages["wo_ssm"])
            act_ret_setup(act)
            act.dma_start(s0r[:, :, :, :], a["s_ret"]).then_inc(S("ld_s0r"), 16)
            act_ret(act)
            act.wait_ge(S("ret_so"), 4)
            act.dma_start(o["s_ret"], soutr[:, :, :, :]).then_inc(S("st_ret"), 16)
            act.wait_ge(S("st_ret"), 16)
            act_ret_out(act)
            act_out_stage(act, stages["wo_ret"], "norm01")
            act_root(act, "norm01")
            act_apply(act, "norm01", gate(0, 3))
            for n in range(3):
                act_up(act, stages[f"up0{n}"], 0)
                act_out_stage(act, stages[f"dn0{n}"], "norm10" if n == 2 else None)
            act_root(act, "norm10")
            act_apply(act, "norm10", gate(1, 0))
            act_qkv(act)
            act.wait_ge(S("pe_unit"), stages["qkv"].u0 + 12)
            act.dma_start(rope[:, :, :, :], a["rope"]).then_inc(S("ld_rope"), 16)
            act_qk(act)
            act.wait_ge(S("at_v"), 3)
            act.dma_start(o["k"], qkv[:, 0, AH * AD:QK]).then_inc(S("st_kv"), 16)
            act.dma_start(o["v"], qkv[:, 0, QK:QK + AG * AD]).then_inc(S("st_kv"), 16)
            act_qkT(act)
            act_att(act)
            act_out_stage(act, stages["wo"], "norm11")
            act_root(act, "norm11")
            act_apply(act, "norm11", gate(1, 3))
            act.wait_ge(S("st_kv"), 32)
            for n in range(3):
                act_up(act, stages[f"up1{n}"], 1)
                act_out_stage(act, stages[f"dn1{n}"])

        @block.vector
        def _(dve):
            dve_setup(dve)
            dve_small(dve)
            for k in range(KT):
                dve_add_square(dve, "norm00", k)
            dve_rstd(dve, "norm00")
            for b in range(MA + 2):
                dve_split(dve, b)
            dve_mod(dve, "modA")
            dve_apply(dve, "norm00", x, gain(0, 0), gate(0, 0))
            dve_dt(dve)
            dve_ssd_in(dve)
            dve_cum(dve)
            dve_ssd(dve)
            dve.wait_ge(S("st_ssm"), 16)
            dve_mod(dve, "modB")
            dve_apply(dve, "again", x, gain(0, 0), gate(0, 0))
            dve_ret_in(dve)
            dve_rstd(dve, "normS")
            dve.wait_ge(S("pe_unit"), stages["g"].u0 + 8)
            dve_apply(dve, "normS", zT, lambda k, g: ssmgain[:, k:k + 1], None)
            dve_out_stage(dve, stages["wo_ssm"], gate(0, 2))
            dve_ret_setup(dve)
            dve_ret(dve)
            dve_ret_out(dve)
            dve_out_stage(dve, stages["wo_ret"], gate(0, 2), "norm01")
            dve_rstd(dve, "norm01")
            dve_apply(dve, "norm01", x, gain(0, 1), gate(0, 3))
            for n in range(3):
                dve_up(dve, stages[f"up0{n}"], 0)
                dve_out_stage(dve, stages[f"dn0{n}"], gate(0, 5), "norm10" if n == 2 else None)
            dve_rstd(dve, "norm10")
            dve_apply(dve, "norm10", x, gain(1, 0), gate(1, 0))
            dve_qkv(dve)
            dve_qk(dve)
            dve_att(dve)
            dve_out_stage(dve, stages["wo"], gate(1, 2), "norm11")
            dve_rstd(dve, "norm11")
            dve_apply(dve, "norm11", x, gain(1, 1), gate(1, 3))
            for n in range(3):
                dve_up(dve, stages[f"up1{n}"], 1)
                dve_out_stage(dve, stages[f"dn1{n}"], gate(1, 5))

        @block.tensor
        def _(pe):
            pe_norm(pe, "norm00")
            pe.wait_ge(S("cond"), 3)
            pe_modA(pe)
            pe_ssd_in(pe)
            pe_cum(pe)
            pe_ssd(pe)
            pe_spread(pe, "again")
            pe_ret_in(pe)
            pe_norm(pe, "normS")
            pe_stage(pe, stages["wo_ssm"], H, hready("normS"))
            pe_ret(pe)
            pe_ret_out(pe)
            pe_stage(pe, stages["wo_ret"], H, hready("retT"))
            pe_norm(pe, "norm01")
            for n in range(3):
                s = stages[f"up0{n}"]
                pe_stage(pe, s, H, hready("norm01") if n == 0 else None)
                pe_stage(pe, stages[f"dn0{n}"], HID, ("hid_ready", s.p0))
            pe_norm(pe, "norm10")
            pe_qkv(pe)
            pe_qkT(pe)
            pe_att(pe)
            pe.wait_ge(S("at_empty"), 1)
            pe.wait_ge(S("at_lo"), NCH * AG)
            pe_stage(pe, stages["wo"], H)
            pe_norm(pe, "norm11")
            for n in range(3):
                s = stages[f"up1{n}"]
                pe_stage(pe, s, H, hready("norm11") if n == 0 else None)
                pe_stage(pe, stages[f"dn1{n}"], HID, ("hid_ready", s.p0))
    return nc


def _tiles(w, cols=128):
    import numpy as np
    k, m = w.shape
    return np.ascontiguousarray(w.reshape(k // 128, 128, m // cols, cols).transpose(2, 1, 0, 3)).reshape(m // cols, 128, -1)


def _mod_units(w):
    import numpy as np
    n = w.shape[1] // 512
    return np.ascontiguousarray(w.reshape(4, 2, 128, n, 512).transpose(3, 0, 2, 1, 4)).reshape(4 * n, 128, 1024)


def _feat(v):
    import numpy as np
    v = v.reshape(v.shape[:-1] + (v.shape[-1] // 128, 128))
    return np.ascontiguousarray(np.moveaxis(v, -1, 0))


def kernel(x_prompt, x_sample, state_ret, state_ssm, cache_attn_k, cache_attn_v, c, c_ctx,
           w_mod, b_mod, norm_mix, norm_ffn, ffn_w_up, ffn_conv_w, ffn_conv_b, ffn_w_down,
           hyb_w_in, hyb_w_out, ret_log_decay, ret_gn_gain, ssm_conv_w, ssm_conv_b, ssm_a_log,
           ssm_dt_bias, ssm_d, ssm_norm_gain, attn_w_qkv, attn_q_gain, attn_k_gain, attn_w_o):
    import numpy as np
    import concourse.bacc as bacc
    from concourse.bass_utils import run_bass_kernel_spmd as run

    f32 = np.float32
    A = {}
    xf = np.zeros((128, KT, TOK), f32)
    xf[:, :, PROMPT[0]:PROMPT[1]] = _feat(x_prompt[0]).transpose(0, 2, 1)
    xf[:, :, SAMPLE[0]:SAMPLE[1]] = _feat(x_sample[0]).transpose(0, 2, 1)
    A["x"] = xf
    A["cond"] = np.ascontiguousarray(_feat(np.stack([c_ctx, c[0]])).transpose(0, 2, 1))
    A["consts"] = constants()
    A["rope"] = rope_tables()
    A["w_modA"] = _mod_units(w_mod[0][:, :2 * D_MODEL])
    A["w_modB"] = _mod_units(np.concatenate([w_mod[0][:, 2 * D_MODEL:], w_mod[1]], 1))
    A["b_mod"] = _feat(b_mod)
    A["norms"] = _feat(np.stack([norm_mix, norm_ffn], 1))
    w = hyb_w_in[0]
    dt = np.zeros((D_MODEL, 128), f32)
    for at in range(0, 128, 32):
        dt[:, at:at + SH] = w[:, 6144:6160]
    A["hyb_in"] = _tiles(np.concatenate([dt, w[:, 4096:6144], w[:, 3072:4096], w[:, 0:3072]], 1))
    A["hyb_out"] = np.stack([_tiles(hyb_w_out[0][h * 1024:(h + 1) * 1024]) for h in range(2)])
    up = ffn_w_up.reshape(2, D_MODEL, 2, FT, 128).transpose(0, 1, 3, 2, 4).reshape(2, D_MODEL, 2 * FFN)
    A["ffn_up"] = np.stack([_tiles(w_) for w_ in up])
    A["ffn_down"] = np.stack([_tiles(w_) for w_ in ffn_w_down])
    fc = np.concatenate([ffn_conv_w, ffn_conv_b[:, None]], 1).reshape(2, 4, 2, FT, 128)
    A["ffn_conv"] = np.ascontiguousarray(fc.transpose(4, 0, 3, 2, 1)).reshape(128, 2, 2 * FT, 4)
    sc = np.concatenate([ssm_conv_w[0], ssm_conv_b], 0).reshape(4, 16, 128)
    A["ssm_conv"] = np.ascontiguousarray(sc.transpose(2, 1, 0))
    A["ssm_gain"] = _feat(ssm_norm_gain[0])
    A["gn_gain"] = _feat(ret_gn_gain[0])
    dp = np.zeros((128, 2), f32)
    for at in range(0, 128, 64):
        for d in range(2):
            dp[at + 32 * d:at + 32 * d + SH, 0] = ssm_dt_bias[0, d]
            if at:
                dp[at + 32 * d:at + 32 * d + SH, 1] = ssm_a_log[0, d]
    A["dt_params"] = dp
    A["decay"] = np.ascontiguousarray(ret_log_decay[0].reshape(16))
    A["decay_pair"] = np.ascontiguousarray(np.repeat(ret_log_decay[0].reshape(2, 4, 2).transpose(2, 0, 1), 64, 0))
    A["ssm_d"] = np.ascontiguousarray(ssm_d[0])
    A["qk_gain"] = np.stack([attn_q_gain[0], attn_k_gain[0]])
    A["qkv"] = _tiles(attn_w_qkv[0])
    A["attn_o"] = _tiles(attn_w_o[0])
    kp = cache_attn_k[0, 0].transpose(2, 1, 0)
    A["k_past"] = np.ascontiguousarray(np.concatenate([kp, kp], 0))
    A["v_past"] = np.ascontiguousarray(cache_attn_v[0, 0].reshape(PAST, AG * AD))
    sr = state_ret[0, 0].reshape(2, 4, 2, 64, 128)
    A["s_ret"] = np.ascontiguousarray(sr.transpose(2, 3, 1, 0, 4)).reshape(128, 4, 2, 128)
    A["s_ssm"] = np.ascontiguousarray(state_ssm[0, 0].transpose(2, 0, 1, 3))

    nc = bacc.Bacc("TRN2", target_bir_lowering=False, num_devices=1, dynamic_dma_scratch_size=1024)
    f = mybir.dt.float32
    ins, arrays = {}, {}
    for name, v in A.items():
        v = np.ascontiguousarray(v, dtype=f32)
        arrays[f"in_{name}"] = v
        ins[name] = nc.dram_tensor(f"in_{name}", v.shape, f, kind="ExternalInput").ap()
    shapes = {"y": (128, KT, TOK), "s_ssm": (128, 2, SH, 64), "s_ret": (128, 2, 4, 128), "k": (128, 256), "v": (128, 256)}
    outs = {n: nc.dram_tensor(f"out_{n}", s, f, kind="ExternalOutput").ap() for n, s in shapes.items()}
    build(nc, ins, outs)
    r = run(nc, [arrays], core_ids=[0]).results[0]
    y = r["out_y"].transpose(2, 1, 0).reshape(TOK, D_MODEL)
    s_ret = r["out_s_ret"].reshape(2, 64, 2, 4, 128).transpose(2, 3, 0, 1, 4).reshape(1, 1, 2, RH, RDK, RDV)
    return (np.ascontiguousarray(y[PROMPT[0]:PROMPT[1]])[None], np.ascontiguousarray(y[SAMPLE[0]:SAMPLE[1]])[None],
            np.ascontiguousarray(s_ret),
            np.ascontiguousarray(r["out_s_ssm"].transpose(1, 2, 0, 3))[None, None],
            r["out_k"].reshape(1, 1, SEQ, AG, AD), r["out_v"].reshape(1, 1, SEQ, AG, AD))
```
